# Optimizing a Trainium2 kernel written in Bass

```python
import jax, jax.numpy as jnp
from jax import lax
import numpy as np

D_MODEL = 1024
BATCH = 1
SEQ = 512
DEPTH = 2
DEC_BATCH = 8
DEC_SEQ = 16
PAST_LEN = 256

CHUNK = 64
N_EVEN = (DEPTH + 1) // 2
N_ODD = DEPTH // 2
RMS_EPS = 1e-6
LN_EPS = 1e-5
CONF_DIM = 512
CONF_WIDTH = 31
SSD_HEADS = 8
SSD_HEAD_DIM = 64
SSD_DIM = SSD_HEADS * SSD_HEAD_DIM
SSD_STATE = 128
SSD_GROUPS = 2
SSD_CONV = 4
SSD_XBC = SSD_DIM + 2 * SSD_GROUPS * SSD_STATE
SSD_CHUNK = CHUNK
EV_PROJ = 2 * CONF_DIM + SSD_DIM + SSD_XBC + SSD_HEADS
EV_MIX = CONF_DIM + SSD_DIM
SC_DIM = 512
SC_WIDTH = 3
FOX_HEADS = 8
FOX_HEAD_DIM = 64
FOX_DIM = FOX_HEADS * FOX_HEAD_DIM
Q_BLOCK = 128
OD_PROJ = 3 * SC_DIM + 3 * FOX_DIM + FOX_HEADS
OD_MIX = SC_DIM + FOX_DIM
MEM_TOKENS = 256
MEM_HEADS = 4
MEM_HEAD_DIM = 128
MEM_DIM = MEM_HEADS * MEM_HEAD_DIM
FFN_DIM = -(-8 * D_MODEL // (3 * 256)) * 256

kernel_name = 'hybrid_stream_encoder_step'

def rmsnorm(x, g, eps=RMS_EPS):
    xf = x.astype(jnp.float32)
    y = xf * lax.rsqrt(jnp.mean(xf * xf, axis=-1, keepdims=True) + eps)
    return (y * g.astype(jnp.float32)).astype(x.dtype)

def layernorm(x, g, b, eps=LN_EPS):
    xf = x.astype(jnp.float32)
    mu = jnp.mean(xf, axis=-1, keepdims=True)
    xc = xf - mu
    var = jnp.mean(xc * xc, axis=-1, keepdims=True)
    return (xc * lax.rsqrt(var + eps) * g.astype(jnp.float32) + b.astype(jnp.float32)).astype(x.dtype)

def causal_dwconv(x, prev, w, b=None):
    width, ch = w.shape
    xp = jnp.concatenate([prev.astype(x.dtype), x], axis=1)
    y = lax.conv_general_dilated(xp, w.astype(x.dtype)[:, None, :], (1,), 'VALID',
                                 dimension_numbers=('NWC', 'WIO', 'NWC'), feature_group_count=ch)
    if b is not None:
        y = y + b.astype(y.dtype)
    return y, xp[:, xp.shape[1] - (width - 1):]

def ssd_scan(x, dt, a, b_in, c_out, h0):
    bsz, seqlen, nh, hd = x.shape
    q = min(SSD_CHUNK, seqlen)
    nc = seqlen // q
    f32 = jnp.float32
    xdt = (x.astype(f32) * dt[..., None]).reshape(bsz, nc, q, nh, hd)
    da = (dt * a).reshape(bsz, nc, q, nh)
    bh = jnp.repeat(b_in.astype(f32), nh // SSD_GROUPS, axis=2).reshape(bsz, nc, q, nh, SSD_STATE)
    chh = jnp.repeat(c_out.astype(f32), nh // SSD_GROUPS, axis=2).reshape(bsz, nc, q, nh, SSD_STATE)
    cs = jnp.cumsum(da, axis=2)
    causal = jnp.tril(jnp.ones((q, q), dtype=bool))
    seg = cs[:, :, :, None, :] - cs[:, :, None, :, :]
    lmat = jnp.exp(jnp.where(causal[None, None, :, :, None], seg, -jnp.inf))
    scores = jnp.einsum('bclhn,bcshn->bclsh', chh, bh) * lmat
    y_diag = jnp.einsum('bclsh,bcshp->bclhp', scores, xdt)
    decay_to_end = jnp.exp(cs[:, :, -1:, :] - cs)
    chunk_states = jnp.einsum('bcshn,bcsh,bcshp->bchpn', bh, decay_to_end, xdt)
    chunk_decay = jnp.exp(cs[:, :, -1, :])

    def step(state, inp):
        st, dec = inp
        return state * dec[:, :, None, None] + st, state

    h_last, h_in = lax.scan(step, h0.astype(f32),
                            (jnp.moveaxis(chunk_states, 1, 0), jnp.moveaxis(chunk_decay, 1, 0)))
    h_in = jnp.moveaxis(h_in, 0, 1)
    y_off = jnp.einsum('bclhn,bchpn,bclh->bclhp', chh, h_in, jnp.exp(cs))
    y = (y_diag + y_off).reshape(bsz, seqlen, nh, hd)
    return y.astype(x.dtype), h_last.astype(h0.dtype)

def mixer_even(h, conf_state, ssd_conv_state, ssd_state, w_in, conf_w, conf_b, ln_g, ln_b,
               xbc_w, xbc_b, dt_bias, a_log, d_skip, gnorm_g, w_out):
    bsz, seqlen, _ = h.shape
    proj = h @ w_in
    a_val, a_gate, z, xbc, dt_raw = jnp.split(
        proj, [CONF_DIM, 2 * CONF_DIM, 2 * CONF_DIM + SSD_DIM, 2 * CONF_DIM + SSD_DIM + SSD_XBC], axis=-1)
    a_glu = a_val * jax.nn.sigmoid(a_gate)
    a_conv, new_conf_state = causal_dwconv(a_glu, conf_state, conf_w, conf_b)
    a_out = jax.nn.silu(layernorm(a_conv, ln_g, ln_b))
    xbc_c, new_xbc_state = causal_dwconv(xbc, ssd_conv_state, xbc_w, xbc_b)
    xbc_c = jax.nn.silu(xbc_c)
    xs, b_in, c_out = jnp.split(xbc_c, [SSD_DIM, SSD_DIM + SSD_GROUPS * SSD_STATE], axis=-1)
    xs = xs.reshape(bsz, seqlen, SSD_HEADS, SSD_HEAD_DIM)
    b_in = b_in.reshape(bsz, seqlen, SSD_GROUPS, SSD_STATE)
    c_out = c_out.reshape(bsz, seqlen, SSD_GROUPS, SSD_STATE)
    dt = jax.nn.softplus(dt_raw.astype(jnp.float32) + dt_bias.astype(jnp.float32))
    a = -jnp.exp(a_log.astype(jnp.float32))
    y, new_ssd_state = ssd_scan(xs, dt, a, b_in, c_out, ssd_state)
    y = y + d_skip.astype(y.dtype)[:, None] * xs
    yg = (y.reshape(bsz, seqlen, SSD_DIM) * jax.nn.silu(z)).reshape(bsz, seqlen, SSD_GROUPS, SSD_DIM // SSD_GROUPS)
    b_out = rmsnorm(yg, gnorm_g.reshape(SSD_GROUPS, SSD_DIM // SSD_GROUPS)).reshape(bsz, seqlen, SSD_DIM)
    out = jnp.concatenate([a_out, b_out], axis=-1) @ w_out
    return out, new_conf_state, new_xbc_state, new_ssd_state

def fox_attention(q, k, v, f_q, f_k, q_start):
    bsz, lq, nh, hd = q.shape
    lk = k.shape[1]
    qb = min(Q_BLOCK, lq)
    nb = lq // qb
    scale = hd ** -0.5
    k_pos = jnp.arange(lk)
    f_kt = jnp.swapaxes(f_k, 1, 2)

    def block(args):
        q_blk, fq_blk, pos_blk = args
        s = jnp.einsum('bqhd,bkhd->bhqk', q_blk, k).astype(jnp.float32) * scale
        s = s + jnp.swapaxes(fq_blk, 1, 2)[..., None] - f_kt[:, :, None, :]
        s = jnp.where(k_pos[None, None, None, :] <= pos_blk[None, None, :, None], s, -jnp.inf)
        p = jax.nn.softmax(s, axis=-1)
        return jnp.einsum('bhqk,bkhd->bqhd', p.astype(v.dtype), v)

    q_blocks = jnp.moveaxis(q.reshape(bsz, nb, qb, nh, hd), 1, 0)
    fq_blocks = jnp.moveaxis(f_q.reshape(bsz, nb, qb, nh), 1, 0)
    pos_blocks = (q_start + jnp.arange(lq)).reshape(nb, qb)
    out = lax.map(block, (q_blocks, fq_blocks, pos_blocks))
    return jnp.moveaxis(out, 0, 1).reshape(bsz, lq, nh, hd)

def mixer_odd(h, sconv_state, past_k, past_v, past_logf, w_in, sconv_w, q_norm_g, k_norm_g, f_bias, w_out):
    bsz, seqlen, _ = h.shape
    proj = h @ w_in
    u, gate_b, gate_c, q, k, v, f_raw = jnp.split(
        proj, [SC_DIM, 2 * SC_DIM, 3 * SC_DIM, 3 * SC_DIM + FOX_DIM, 3 * SC_DIM + 2 * FOX_DIM,
               3 * SC_DIM + 3 * FOX_DIM], axis=-1)
    conv, new_sconv_state = causal_dwconv(gate_c * u, sconv_state, sconv_w)
    c_out = gate_b * conv
    q = rmsnorm(q.reshape(bsz, seqlen, FOX_HEADS, FOX_HEAD_DIM), q_norm_g)
    k = rmsnorm(k.reshape(bsz, seqlen, FOX_HEADS, FOX_HEAD_DIM), k_norm_g)
    v = v.reshape(bsz, seqlen, FOX_HEADS, FOX_HEAD_DIM)
    logf = jax.nn.log_sigmoid(f_raw.astype(jnp.float32) + f_bias.astype(jnp.float32))
    past_len = past_k.shape[1]
    k_all = jnp.concatenate([past_k.astype(k.dtype), k], axis=1)
    v_all = jnp.concatenate([past_v.astype(v.dtype), v], axis=1)
    f_cum = jnp.cumsum(jnp.concatenate([past_logf.astype(jnp.float32), logf], axis=1), axis=1)
    d_out = fox_attention(q, k_all, v_all, f_cum[:, past_len:], f_cum, past_len)
    out = jnp.concatenate([c_out, d_out.reshape(bsz, seqlen, FOX_DIM)], axis=-1) @ w_out
    return out, new_sconv_state, k, v, logf.astype(h.dtype)

def mem_kv(mem, norm_g, wk, wv, k_norm_g):
    bsz, m, _ = mem.shape
    hm = rmsnorm(mem, norm_g)
    mk = rmsnorm((hm @ wk).reshape(bsz, m, MEM_HEADS, MEM_HEAD_DIM), k_norm_g)
    mv = (hm @ wv).reshape(bsz, m, MEM_HEADS, MEM_HEAD_DIM)
    return mk, mv

def cross_attn(h, wq, q_norm_g, mk, mv, wo):
    bsz, seqlen, _ = h.shape
    q = rmsnorm((h @ wq).reshape(bsz, seqlen, MEM_HEADS, MEM_HEAD_DIM), q_norm_g)
    s = jnp.einsum('blhd,bmhd->bhlm', q, mk.astype(q.dtype)).astype(jnp.float32) * (MEM_HEAD_DIM ** -0.5)
    p = jax.nn.softmax(s, axis=-1)
    o = jnp.einsum('bhlm,bmhd->blhd', p.astype(h.dtype), mv.astype(h.dtype))
    return o.reshape(bsz, seqlen, MEM_DIM) @ wo

def swiglu(h, w1, w3, w2):
    return (jax.nn.silu(h @ w1) * (h @ w3)) @ w2

def setup_inputs(seed: int = 0) -> dict:
    key = jax.random.key(seed)
    ks = iter(jax.random.split(key, 64))

    def nrm(shape, scale):
        return jax.random.normal(next(ks), shape, jnp.float32) * scale

    def gain(shape):
        return 1.0 + nrm(shape, 0.05)

    dt0 = jnp.exp(jax.random.uniform(next(ks), (N_EVEN, SSD_HEADS), jnp.float32,
                                     minval=float(np.log(1e-3)), maxval=float(np.log(1e-1))))
    return {
        'x_prompt': nrm((BATCH, SEQ, D_MODEL), 1.0),
        'x_sample': nrm((DEC_BATCH, DEC_SEQ, D_MODEL), 1.0),
        'state_conf_conv': nrm((N_EVEN, DEC_BATCH, CONF_WIDTH - 1, CONF_DIM), 0.5),
        'state_ssd_conv': nrm((N_EVEN, DEC_BATCH, SSD_CONV - 1, SSD_XBC), 0.5),
        'state_ssd': nrm((N_EVEN, DEC_BATCH, SSD_HEADS, SSD_HEAD_DIM, SSD_STATE), 0.1),
        'state_sconv': nrm((N_ODD, DEC_BATCH, SC_WIDTH - 1, SC_DIM), 0.5),
        'cache_fox_k': nrm((N_ODD, DEC_BATCH, PAST_LEN, FOX_HEADS, FOX_HEAD_DIM), 1.0),
        'cache_fox_v': nrm((N_ODD, DEC_BATCH, PAST_LEN, FOX_HEADS, FOX_HEAD_DIM), 1.0),
        'cache_fox_logf': jax.nn.log_sigmoid(2.5 + nrm((N_ODD, DEC_BATCH, PAST_LEN, FOX_HEADS), 1.0)),
        'cache_mem_k': nrm((DEPTH, DEC_BATCH, MEM_TOKENS, MEM_HEADS, MEM_HEAD_DIM), 1.0),
        'cache_mem_v': nrm((DEPTH, DEC_BATCH, MEM_TOKENS, MEM_HEADS, MEM_HEAD_DIM), 1.0),
        'mem_prompt': nrm((BATCH, MEM_TOKENS, D_MODEL), 1.0),
        'norm_mix_g': gain((DEPTH, D_MODEL)),
        'norm_cross_g': gain((DEPTH, D_MODEL)),
        'norm_mem_g': gain((DEPTH, D_MODEL)),
        'norm_ffn_g': gain((DEPTH, D_MODEL)),
        'ev_w_in': nrm((N_EVEN, D_MODEL, EV_PROJ), D_MODEL ** -0.5),
        'ev_w_out': nrm((N_EVEN, EV_MIX, D_MODEL), EV_MIX ** -0.5),
        'conf_dw_w': nrm((N_EVEN, CONF_WIDTH, CONF_DIM), CONF_WIDTH ** -0.5),
        'conf_dw_b': nrm((N_EVEN, CONF_DIM), 0.02),
        'conf_ln_g': gain((N_EVEN, CONF_DIM)),
        'conf_ln_b': nrm((N_EVEN, CONF_DIM), 0.02),
        'ssd_conv_w': nrm((N_EVEN, SSD_CONV, SSD_XBC), SSD_CONV ** -0.5),
        'ssd_conv_b': nrm((N_EVEN, SSD_XBC), 0.02),
        'ssd_dt_bias': dt0 + jnp.log(-jnp.expm1(-dt0)),
        'ssd_a_log': jnp.log(jax.random.uniform(next(ks), (N_EVEN, SSD_HEADS), jnp.float32, minval=1.0, maxval=16.0)),
        'ssd_d': gain((N_EVEN, SSD_HEADS)),
        'ssd_norm_g': gain((N_EVEN, SSD_DIM)),
        'od_w_in': nrm((N_ODD, D_MODEL, OD_PROJ), D_MODEL ** -0.5),
        'od_w_out': nrm((N_ODD, OD_MIX, D_MODEL), OD_MIX ** -0.5),
        'sconv_w': nrm((N_ODD, SC_WIDTH, SC_DIM), SC_WIDTH ** -0.5),
        'fox_q_norm_g': gain((N_ODD, FOX_HEAD_DIM)),
        'fox_k_norm_g': gain((N_ODD, FOX_HEAD_DIM)),
        'fox_f_bias': jax.random.uniform(next(ks), (N_ODD, FOX_HEADS), jnp.float32, minval=1.0, maxval=4.0),
        'xa_wq': nrm((DEPTH, D_MODEL, MEM_DIM), D_MODEL ** -0.5),
        'xa_wk': nrm((DEPTH, D_MODEL, MEM_DIM), D_MODEL ** -0.5),
        'xa_wv': nrm((DEPTH, D_MODEL, MEM_DIM), D_MODEL ** -0.5),
        'xa_wo': nrm((DEPTH, MEM_DIM, D_MODEL), MEM_DIM ** -0.5),
        'xa_q_norm_g': gain((DEPTH, MEM_HEAD_DIM)),
        'xa_k_norm_g': gain((DEPTH, MEM_HEAD_DIM)),
        'ffn_w1': nrm((DEPTH, D_MODEL, FFN_DIM), D_MODEL ** -0.5),
        'ffn_w3': nrm((DEPTH, D_MODEL, FFN_DIM), D_MODEL ** -0.5),
        'ffn_w2': nrm((DEPTH, FFN_DIM, D_MODEL), FFN_DIM ** -0.5),
    }

def reference(x_prompt, x_sample, state_conf_conv, state_ssd_conv, state_ssd, state_sconv,
              cache_fox_k, cache_fox_v, cache_fox_logf, cache_mem_k, cache_mem_v, mem_prompt,
              norm_mix_g, norm_cross_g, norm_mem_g, norm_ffn_g,
              ev_w_in, ev_w_out, conf_dw_w, conf_dw_b, conf_ln_g, conf_ln_b,
              ssd_conv_w, ssd_conv_b, ssd_dt_bias, ssd_a_log, ssd_d, ssd_norm_g,
              od_w_in, od_w_out, sconv_w, fox_q_norm_g, fox_k_norm_g, fox_f_bias,
              xa_wq, xa_wk, xa_wv, xa_wo, xa_q_norm_g, xa_k_norm_g,
              ffn_w1, ffn_w3, ffn_w2):
    yp, ys = x_prompt, x_sample
    bp, dt_ = x_prompt.shape[0], x_prompt.dtype
    conf_p, conf_s, xbc_p, xbc_s, ssd_p, ssd_s = [], [], [], [], [], []
    sc_p, sc_s, fk_p, fk_s, fv_p, fv_s, fl_p, fl_s = [], [], [], [], [], [], [], []
    mk_out, mv_out = [], []
    for l in range(DEPTH):
        g = l // 2
        hp = rmsnorm(yp, norm_mix_g[l])
        hs = rmsnorm(ys, norm_mix_g[l])
        if l % 2 == 0:
            w_ev = (ev_w_in[g], conf_dw_w[g], conf_dw_b[g], conf_ln_g[g], conf_ln_b[g], ssd_conv_w[g],
                    ssd_conv_b[g], ssd_dt_bias[g], ssd_a_log[g], ssd_d[g], ssd_norm_g[g], ev_w_out[g])
            mp, c1, c2, c3 = mixer_even(hp, jnp.zeros((bp, CONF_WIDTH - 1, CONF_DIM), dt_),
                                        jnp.zeros((bp, SSD_CONV - 1, SSD_XBC), dt_),
                                        jnp.zeros((bp, SSD_HEADS, SSD_HEAD_DIM, SSD_STATE), dt_), *w_ev)
            ms, s1, s2, s3 = mixer_even(hs, state_conf_conv[g], state_ssd_conv[g], state_ssd[g], *w_ev)
            conf_p.append(c1); xbc_p.append(c2); ssd_p.append(c3)
            conf_s.append(s1); xbc_s.append(s2); ssd_s.append(s3)
        else:
            w_od = (od_w_in[g], sconv_w[g], fox_q_norm_g[g], fox_k_norm_g[g], fox_f_bias[g], od_w_out[g])
            mp, c1, c2, c3, c4 = mixer_odd(hp, jnp.zeros((bp, SC_WIDTH - 1, SC_DIM), dt_),
                                           jnp.zeros((bp, 0, FOX_HEADS, FOX_HEAD_DIM), dt_),
                                           jnp.zeros((bp, 0, FOX_HEADS, FOX_HEAD_DIM), dt_),
                                           jnp.zeros((bp, 0, FOX_HEADS), dt_), *w_od)
            ms, s1, s2, s3, s4 = mixer_odd(hs, state_sconv[g], cache_fox_k[g], cache_fox_v[g],
                                           cache_fox_logf[g], *w_od)
            sc_p.append(c1); fk_p.append(c2); fv_p.append(c3); fl_p.append(c4)
            sc_s.append(s1); fk_s.append(s2); fv_s.append(s3); fl_s.append(s4)
        yp = yp + mp
        ys = ys + ms
        mkp, mvp = mem_kv(mem_prompt, norm_mem_g[l], xa_wk[l], xa_wv[l], xa_k_norm_g[l])
        mk_out.append(mkp); mv_out.append(mvp)
        yp = yp + cross_attn(rmsnorm(yp, norm_cross_g[l]), xa_wq[l], xa_q_norm_g[l], mkp, mvp, xa_wo[l])
        ys = ys + cross_attn(rmsnorm(ys, norm_cross_g[l]), xa_wq[l], xa_q_norm_g[l],
                             cache_mem_k[l], cache_mem_v[l], xa_wo[l])
        yp = yp + swiglu(rmsnorm(yp, norm_ffn_g[l]), ffn_w1[l], ffn_w3[l], ffn_w2[l])
        ys = ys + swiglu(rmsnorm(ys, norm_ffn_g[l]), ffn_w1[l], ffn_w3[l], ffn_w2[l])
    new_conf_conv_p = jnp.stack(conf_p)
    new_conf_conv_s = jnp.stack(conf_s)
    new_ssd_conv_p = jnp.stack(xbc_p)
    new_ssd_conv_s = jnp.stack(xbc_s)
    new_ssd_p = jnp.stack(ssd_p)
    new_ssd_s = jnp.stack(ssd_s)
    new_sconv_p = jnp.stack(sc_p)
    new_sconv_s = jnp.stack(sc_s)
    new_fox_k_p = jnp.stack(fk_p)
    new_fox_k_s = jnp.stack(fk_s)
    new_fox_v_p = jnp.stack(fv_p)
    new_fox_v_s = jnp.stack(fv_s)
    new_fox_logf_p = jnp.stack(fl_p)
    new_fox_logf_s = jnp.stack(fl_s)
    new_mem_k_p = jnp.stack(mk_out)
    new_mem_v_p = jnp.stack(mv_out)
    return (yp, ys, new_conf_conv_p, new_conf_conv_s, new_ssd_conv_p, new_ssd_conv_s, new_ssd_p, new_ssd_s,
            new_sconv_p, new_sconv_s, new_fox_k_p, new_fox_k_s, new_fox_v_p, new_fox_v_s,
            new_fox_logf_p, new_fox_logf_s, new_mem_k_p, new_mem_v_p)


_drawn_inputs = setup_inputs


def setup_inputs(seed=0):
    import zlib

    import numpy as np

    out = dict(_drawn_inputs(seed))
    spreads = {}
    factors = {'cache_fox_logf': 3.237,
     'norm_cross_g': 8.0,
     'conf_dw_b': 2.901,
     'conf_ln_b': 5.028,
     'ssd_d': 3.0,
     'fox_q_norm_g': 8.0,
     'xa_q_norm_g': 8.0}
    for name, (base, spread) in spreads.items():
        noise = np.random.default_rng([zlib.crc32(name.encode()), seed]).standard_normal(out[name].shape)
        drawn = base * np.exp(spread * noise) if base else spread * noise
        out[name] = __import__('jax').numpy.asarray(drawn.astype(out[name].dtype))
    for name, factor in factors.items():
        out[name] = (out[name] * factor).astype(out[name].dtype)
    return out
```

```python
from contextlib import ExitStack

import numpy as np

import concourse.bass as bass
from concourse import mybir

F32 = mybir.dt.float32
F32R = mybir.dt.float32r
ALU = mybir.AluOpType
ACT = mybir.ActivationFunctionType
AX_X = mybir.AxisListType.X

P = 128
D = 1024
KD = D // P
SEQ, REQ, STEP = 512, 8, 16
NS = REQ * STEP
T = SEQ + NS
PAST = 256
HID = 2816
KH = HID // P
HALF = KH // 2
KS = 6
CONF, CW = 512, 31
XBC, XW = 1024, 4
SC, SW = 512, 3
NH = 8
HD = 64
MH, MT = 4, 256
CPROMPT, CREQ = CW - 1 + SEQ, CW - 1 + STEP
CONF_ROW = CPROMPT + REQ * CREQ
XPROMPT, XREQ = XW - 1 + SEQ, XW - 1 + STEP
XBC_ROW = XPROMPT + REQ * XREQ
SPROMPT, SREQ = SW - 1 + SEQ, SW - 1 + STEP
SC_ROW = SPROMPT + REQ * SREQ
NCH = T // P
NSEG = SEQ // P + REQ
KALL = PAST + STEP
NEG = -1e30
RING = 4
WCH = 2048
LAYERS = 2

CONST = {}


def _place(table, name, n):
    table[name] = (table.get("_", 0), n)
    table["_"] = table.get("_", 0) + n


for _n, _w in (("ident", P), ("ones", P), ("half", P), ("cmask", P), ("lmask", P), ("smask", P),
               ("d8", NH), ("nd8", NH), ("sel", 4 * P), ("nd16", P), ("req", REQ), ("negwin", 240), ("r16", P), ("m16", STEP)):
    _place(CONST, _n, _w)
PAR = {}
for _n, _w in (("mix0", KD), ("mix1", KD), ("cross0", KD), ("cross1", KD), ("mem0", KD), ("mem1", KD),
               ("ffn0", KD), ("ffn1", KD), ("cw", 4 * CW), ("cb", 4), ("lng", 4), ("lnb", 4),
               ("xw", KD * XW), ("xb", KD), ("gn", 4), ("sw", 4 * SW), ("fq", 1), ("fk", 1),
               ("xq0", 1), ("xq1", 1), ("xk0", 1), ("xk1", 1), ("dskip", 4),
               ("dtb", 1), ("alog", 1), ("fb", 1), ("wdt", KD * NH), ("wf", KD * NH)):
    _place(PAR, _n, _w)

SCAN_TILES = 5 * (NCH - 1) + 4 + REQ
TILE = {}
for _n, _c in (("glu", 8), ("mk0", 4), ("mv0", 2), ("mk1", 4), ("mv1", 2), ("xbc", 8), ("dt", 1), ("z", 4),
               ("tok", 2), ("scan", SCAN_TILES), ("evout", 8),
               ("q0", 4), ("xo0", 10), ("wo0", 8), ("up0a", KH), ("down0a", 8), ("up0b", KH), ("down0b", 8),
               ("cgu", 8), ("f", 1), ("gb", 4), ("fqk", 8), ("fv", NCH),
               ("fo", 4 * NH + REQ), ("odout", 8),
               ("q1", 4), ("xo1", 10), ("wo1", 8), ("up1a", KH), ("down1a", 8), ("up1b", KH), ("down1b", 8)):
    _place(TILE, _n, _c)
TILE0 = {k: v[0] for k, v in TILE.items() if k != "_"}

APPLIED, NORM, _a, _m = {}, [], 0, 0
for _n, _c in ([("mix0", 8), ("mem", 16)] + [(f"mk{l}.{j}", 0) for l in range(2) for j in range(4)]
               + [("mean", 4), ("var", 4), ("gn0", 2), ("gn1", 2), ("cross0", 8)]
               + [(f"q0.{j}", 1) for j in range(4)] + [("ffn0", 8), ("mix1", 8)]
               + [(f"fqk.{j}", 1) for j in range(8)] + [("cross1", 8)]
               + [(f"q1.{j}", 1) for j in range(4)] + [("ffn1", 8)]):
    _a, _m = _a + _c, _m + (_c == 0)
    APPLIED[_n] = _a
    NORM.append((_c == 0, _m if _c == 0 else _a))


def summed(m):
    return m + 1 + (4 if m >= 24 else 0)


CHUNKS, CHUNK, PIECE0 = [], {}, {"_": 0}


def _chunks(name, count, width, ends):
    CHUNK[name] = len(CHUNKS)
    CHUNKS.extend(("w_" + name, i, width, ends(i)) for i in range(count))


def _pairs(tile):
    return lambda i: TILE0[tile] + 2 * i + 2


def _cross_ffn(l):
    _chunks("q" + l, 2, WCH, _pairs("q" + l))
    _chunks("wo" + l, 4, 4 * 256, _pairs("wo" + l))
    for half in "ab":
        for name in ("up" + l + half, "down" + l + half):
            PIECE0[name] = PIECE0["_"]
            count, width = (HALF, WCH) if name[0] == "u" else (KD, HALF * P)
            PIECE0["_"] += 2 * count
            _chunks(name, count, width, lambda i: -(PIECE0[name] + 2 * i + 2))


_chunks("glu", 4, WCH, _pairs("glu"))
for _l in "01":
    _chunks("mk" + _l, 2, WCH, _pairs("mk" + _l))
    _chunks("mv" + _l, 2, WCH, lambda i, t="mv" + _l: TILE0[t] + 2)
_chunks("xbc", 4, WCH, _pairs("xbc"))
_chunks("z", 2, WCH, _pairs("z"))
_chunks("evout", 4, WCH, _pairs("evout"))
_cross_ffn("0")
_chunks("cgu", 4, WCH, _pairs("cgu"))
_chunks("gb", 2, WCH, _pairs("gb"))
_chunks("fqk", 4, WCH, _pairs("fqk"))
_chunks("fv", 2, WCH, lambda i: TILE0["fv"] + NCH)
_chunks("odout", 4, WCH, _pairs("odout"))
_cross_ffn("1")

FOX_ITEMS = [(h, qt) for h in range(NH) for qt in range(4)]
NFOX = 4 * NH + REQ
NX = 10
SCALE_X = 128 ** -0.5


def build(nc, dram):
    ctx = ExitStack()
    with ctx:
        def sb(name, shape):
            return ctx.enter_context(nc.sbuf_tensor(name, shape, F32))

        def sem(name):
            return ctx.enter_context(nc.semaphore(name))

        const = sb("const", [P, CONST["_"]])
        par = sb("par", [P, PAR["_"]])

        def cst(name, rows=P):
            o, n = CONST[name]
            return const[0:rows, o:o + n]

        def pr(name, i=0, rows=P):
            o = PAR[name][0] + i
            return par[0:rows, o:o + 1]

        x = sb("resid", [P, KD, T])
        ring = sb("ring", [P, RING, WCH])
        sq = sb("sq", [P, 2, T])
        rstd = sb("rstd", [P, 2, T])
        tmp = sb("tmp", [P, 2, T])
        mkT = sb("mkT", [P, LAYERS, MH, MT])
        mv = sb("mv", [P, LAYERS, 2, 512])
        small = sb("small", [P, 8])
        stats = sb("stats", [P, 2, 8])
        csend = sb("csend", [NH, NSEG])
        cdiag = sb("cdiag", [NH, NSEG, NH])
        decay = sb("decay", [P, NSEG, NH])
        toks = sb("toks", [P, 2, NCH, NH])
        ARENA = 24064
        with nc.sbuf_tensor("h", [P, KD, T], F32) as h:
            with nc.sbuf_tensor("arena", [P, ARENA], F32) as arena:
                pass
        hs = ctx.enter_context(nc.sbuf_tensor("h_split", [P, 2, KD, T], F32R))
        gs = ctx.enter_context(nc.sbuf_tensor("g_split", [P, 2, HALF, T], F32R))
        ws = ctx.enter_context(nc.sbuf_tensor("w_split", [P, 2, 2, KD * P], F32R))
        assert 2 * KD * T + 2 * HALF * T + 4 * KD * P <= KD * T + ARENA

        class Region:

            def __init__(self, at=0):
                self.at = at

            def __call__(self, *shape, rows=P):
                n = int(np.prod(shape))
                v = arena[0:rows, self.at:self.at + n]
                self.at += n
                assert self.at <= ARENA, self.at
                names = "abcd"[:len(shape)]
                if len(shape) > 1:
                    v = v.rearrange(f"p ({' '.join(names)}) -> p {' '.join(names)}",
                                    **{c: s for c, s in zip(names[1:], shape[1:])})
                return v

        r = Region()
        aglu = r(4, CONF_ROW)
        xbcp = r(KD, XBC_ROW)
        scan_room = r.at
        zs = r(4, T)
        memx = arena[:, scan_room:scan_room + KD * MT].rearrange("p (k m) -> p k m", k=KD)
        acc = r(4, T)
        xbcc = r(KD, T)
        xbcc_at = r.at - KD * T
        memh = arena[:, xbcc_at:xbcc_at + LAYERS * KD * MT].rearrange("p (l k m) -> p l k m", l=LAYERS, k=KD)
        hT = r(512)
        xdt = r(512)
        xdte = r(512)
        btok = r(256)
        dtb = r(4, T, rows=NH)
        r = Region()
        h0T = r(REQ, 512)
        bmask = r(REQ, 256)
        Lm = r(NH, P)
        ysc = r(4, P)
        assert r.at <= scan_room
        r = Region(scan_room + 4 * T)
        Pm = r(NH, P)
        Ee = r(4, P)
        assert r.at <= xbcc_at
        r = Region()
        cgu = r(4, SC_ROW)
        cacc = r(4, T)
        fqk = r(8, T)
        fv = r(NCH, 512)
        kc = r(2, 4, PAST)
        vc = r(2, 2, 512)
        qblk = r(2, 640)
        flog = r(REQ, KALL, rows=NH)
        fcr = r(REQ, KALL, rows=NH)
        fcp = r(SEQ, rows=NH)
        fl = r(T, rows=NH)
        fqd = r(2, NH, STEP, rows=NH)
        r = Region()
        xq = r(4, T)
        xo = r(4, T)
        xkc = r(4, 2, MH, MT)
        xvc = r(4, 2, 2, 512)
        xqb = r(REQ, 320)
        sqf, tmpf = (t[:, :, :].rearrange("p a b -> p (a b)")[:, 0:1024] for t in (sq, tmp))
        fP = sqf.rearrange("p (b m) -> p b m", b=2)
        fPT = tmpf.rearrange("p (b k m) -> p b k m", b=2, k=4)
        xP = sqf.rearrange("p (b s m) -> p b s m", b=2, s=2)
        xPT = fPT
        G = [ctx.enter_context(nc.psum_tensor(f"G{i}", [P, 1024], F32)) for i in range(2)]
        S = ctx.enter_context(nc.psum_tensor("S", [P, 2, 512], F32))
        Q = ctx.enter_context(nc.psum_tensor("Q", [P, 2, 512], F32))
        QF = Q[:, :, :].rearrange("p a b -> p (a b)")
        HT = T // 2
        GF = [G[i][:, 512 - HT:512 + HT] for i in range(2)]

        high, split = sem("high"), sem("split")
        half_used = sem("half_used")
        h_raw, h_hi = sem("h_raw"), sem("h_hi")
        const_in, x_in, mem_in, pads_in = sem("const_in"), sem("x_in"), sem("mem_in"), sem("pads_in")
        chunk_in = [sem(f"chunk_in{i}") for i in range(RING)]
        tile_done = sem("tile_done")
        read = [sem(f"read{i}") for i in range(2)]
        S_done, Q_done = sem("S_done"), sem("Q_done")
        S_read = [sem(f"S_read{i}") for i in range(2)]
        Q_read = [sem(f"Q_read{i}") for i in range(2)]
        act_self, dve_self = sem("act_self"), sem("dve_self")
        sq_ready, sq_used = sem("sq_ready"), sem("sq_used")
        stat_read, rstd_ready = sem("stat_read"), sem("rstd_ready")
        applied = sem("applied")
        mk_applied, pool_self = sem("mk_applied"), sem("pool_self")
        small_ready, outs = sem("small_ready"), sem("outs")
        conv, xconv, xbc_done = sem("conv"), sem("xconv"), sem("xbc_done")
        mixed = sem("mixed")
        dt_abs, dt_log, cs_ready, de_ready = map(sem, ("dt_abs", "dt_log", "cs_ready", "de_ready"))
        state_in, xdte_ready, gated, hT_zero = map(sem, ("state_in", "xdte_ready", "gated", "hT_zero"))
        neg_ready, prob_ready, qblk_ready = map(sem, ("neg_ready", "prob_ready", "qblk_ready"))
        keys_in = [sem(f"keys_in{i}") for i in range(2)]
        values_in = [sem(f"values_in{i}") for i in range(2)]
        xcache_in = [sem(f"xcache_in{i}") for i in range(4)]
        sc_in, flog_in, f_abs, f_log, f_ready, fcum_ready, gbc = map(
            sem, ("sc_in", "flog_in", "f_abs", "f_log", "f_ready", "fcum_ready", "gbc"))

        block = ctx.enter_context(nc.Block())

        CONV_OUTS = 8 + 16
        SCAN_OUTS = CONV_OUTS + 2 + 2
        ODD_OUTS = SCAN_OUTS + 8 + 3

        def tile_wait(eng, n):
            eng.wait_ge(tile_done, n + 1)

        def read_wait(eng, n):
            eng.wait_ge(read[n % 2], n // 2 + 1)

        def padded(buf, j, pad, prompt, req, off):
            a = buf[:, j, off:off + SEQ]
            b = buf[:, j, prompt:prompt + REQ * req].rearrange("p (r t) -> p r t", r=REQ)
            return a, b[:, :, off:off + STEP]

        def raw_tile(k):
            return (tmp, sq)[k // 2 % 2][:, k % 2, :]

        def piece(name, u, s):
            up = name[0] == "u"
            w = ring[:, (CHUNK[name] + u) % RING, 0:WCH if up else HALF * P]\
                .rearrange("p (k n) -> p k n", k=KD if up else HALF)
            src = w[:, :, s * P:(s + 1) * P] if up else w[:, s * KS:HALF if s else KS]
            KT = src.shape[1]
            parts = [ws[:, s, part, 0:KT * P].rearrange("p (k n) -> p k n", k=KT) for part in range(2)]
            return src, parts[0], parts[1]

        def runs(ap):
            return ap.rearrange("p (r t) -> p r t", r=REQ)

        @block.sync
        def _(sp):
            sp.dma_start(par[:, :], dram["par"]).then_inc(const_in, 16)
            sp.dma_start(const[:, :], dram["const"]).then_inc(const_in, 16)
            sp.dma_start(x[:, :, :], dram["x"]).then_inc(x_in, 16)

            def load(c, idx, free):
                array, _, width, _ = CHUNKS[c]
                if free is not None:
                    done, count = free
                    sp.wait_ge(done, count)
                sp.dma_start(ring[:, c % RING, 0:width], dram[array][idx].rearrange("a p n -> (a p) n"))\
                    .then_inc(chunk_in[c % RING], 16)

            def slot_free(c):
                if c < RING:
                    return None
                count = CHUNKS[c - RING][3]
                return (tile_done, count) if count > 0 else (split, -count)

            c = 0
            while c < len(CHUNKS):
                name, idx = CHUNKS[c][0][2:], CHUNKS[c][1]
                if name in PIECE0:
                    count = HALF if name[0] == "u" else KD
                    for u in range(RING):
                        load(c + u, slice(u, u + 1), slot_free(c + u))
                    loops = count // RING
                    with sp.Fori(1, loops) as i:
                        for u in range(RING):
                            load(c + u, bass.ds(i * RING + u, 1),
                                 (split, i * (2 * RING) + (PIECE0[name] + 2 * (u + 1 - RING))))
                    for u in range(loops * RING, count):
                        load(c + u, slice(u, u + 1), slot_free(c + u))
                    c += count
                else:
                    load(c, slice(idx, idx + 1), slot_free(c))
                    c += 1

        @block.gpsimd
        def _(pool):
            stores = [0]

            def store(dst, src):
                pool.dma_start(dst, src).then_inc(outs, 16)
                stores[0] += 1

            def stores_landed():
                pool.wait_ge(outs, 16 * stores[0])

            pool.dma_start(memx, dram["mem"]).then_inc(mem_in, 16)
            for j in range(4):
                pool.dma_start(aglu[:, j, CPROMPT:].rearrange("p (r t) -> p r t", r=REQ)[:, :, 0:CW - 1],
                               dram["conf_state"][:, j]).then_inc(pads_in, 16)
            for j in range(KD):
                pool.dma_start(xbcp[:, j, XPROMPT:].rearrange("p (r t) -> p r t", r=REQ)[:, :, 0:XW - 1],
                               dram["xbc_state"][:, j]).then_inc(pads_in, 16)
            pool.wait_ge(pads_in, 16 * 12)
            for j in range(4):
                read_wait(pool, TILE0["glu"] + 2 * j + 1)
                store(dram["o_conf_p"][:, j], aglu[:, j, SEQ:SEQ + CW - 1])
                store(dram["o_conf_s"][:, j], aglu[:, j, CPROMPT:].rearrange(
                    "p (r t) -> p r t", r=REQ)[:, :, STEP:])
            for i in range(LAYERS * MH):
                key = mkT[:, i // MH, i % MH, :]
                pool.wait_ge(rstd_ready, i + 3)
                nc.gpsimd.tensor_tensor(key, key, rstd[:, i % 2, 0:MT], ALU.mult).then_inc(pool_self, 1)
                pool.wait_ge(pool_self, i + 1)
                nc.gpsimd.tensor_scalar(key, key, pr(f"xk{i // MH}"), 1.0, ALU.mult, ALU.mult)\
                    .then_inc(mk_applied, 1)
            for j in range(KD):
                read_wait(pool, TILE0["xbc"] + j)
                store(dram["o_xbc_p"][:, j], xbcp[:, j, SEQ:SEQ + XW - 1])
                store(dram["o_xbc_s"][:, j], xbcp[:, j, XPROMPT:].rearrange(
                    "p (r t) -> p r t", r=REQ)[:, :, STEP:])
            stores_landed()
            pool.wait_ge(xbc_done, KD)
            pool.dma_start(h0T, dram["ssd_state"]).then_inc(state_in, 16)
            pool.wait_ge(mk_applied, LAYERS * MH)
            store(dram["o_mk"], mkT[:, :, :, :])
            read_wait(pool, TILE0["mv1"])
            read_wait(pool, TILE0["mv1"] + 1)
            store(dram["o_mv"], mv[:, :, :, :])
            last = TILE0["scan"] + SCAN_TILES - 1
            read_wait(pool, TILE0["scan"] + 5 * (NCH - 1) - 1)
            store(dram["o_ssd_p"], hT)
            read_wait(pool, last)
            read_wait(pool, last - 1)
            store(dram["o_ssd_s"], h0T)
            stores_landed()
            assert stores[0] == SCAN_OUTS

            def cross_caches(l, after):
                tile_wait(pool, after)
                for n in range(4):
                    pool.dma_start(xkc[:, n], dram["mem_k"][l, n]).then_inc(xcache_in[n], 16)
                    pool.dma_start(xvc[:, n], dram["mem_v"][l, n]).then_inc(xcache_in[n], 16)

            cross_caches(0, TILE0["evout"])
            tile_wait(pool, TILE0["cgu"])
            for j in range(4):
                pool.dma_start(cgu[:, j, SPROMPT:].rearrange("p (r t) -> p r t", r=REQ)[:, :, 0:SW - 1],
                               dram["sc_state"][:, j]).then_inc(sc_in, 16)
            pool.dma_start(flog[:, :, 0:PAST], dram["fox_logf"]).then_inc(flog_in, 16)

            def fox_caches(rq):
                if rq >= 2:
                    pool.wait_ge(S_done, 2 * NCH + NX + 4 * NH + rq - 1)
                pool.dma_start(kc[:, rq % 2], dram["fox_k"][rq]).then_inc(keys_in[rq % 2], 16)
                if rq >= 2:
                    tile_wait(pool, TILE0["fo"] + 4 * NH + rq - 2)
                pool.dma_start(vc[:, rq % 2], dram["fox_v"][rq]).then_inc(values_in[rq % 2], 16)

            fox_caches(0)
            fox_caches(1)
            pool.wait_ge(sc_in, 16 * 4)
            for j in range(4):
                read_wait(pool, TILE0["cgu"] + 2 * j + 1)
                store(dram["o_sc_p"][:, j], cgu[:, j, SEQ:SEQ + SW - 1])
                store(dram["o_sc_s"][:, j], cgu[:, j, SPROMPT:].rearrange(
                    "p (r t) -> p r t", r=REQ)[:, :, STEP:])
            pool.wait_ge(applied, APPLIED["fqk.7"])
            store(dram["o_fk"], fqk[:, 4:8, :])
            for c in range(NCH):
                read_wait(pool, TILE0["fv"] + c)
            store(dram["o_fv"], fv)
            pool.wait_ge(f_ready, 1)
            store(dram["o_fl"], fl)
            for rq in range(2, REQ):
                fox_caches(rq)
            stores_landed()
            assert stores[0] == ODD_OUTS
            cross_caches(1, TILE0["odout"] + 7)
            for j in range(KD):
                read_wait(pool, TILE0["down1b"] + j)
                store(dram["o_y"][:, j], x[:, j, :])
            stores_landed()

        @block.tensor
        def _(pe):
            nsq, nready, nstat = [0], [0], [0]
            nS, nQ = [0, 0], [0, 0]

            def mm(out, lhsT, rhs, start, stop, **kw):
                return nc.tensor.matmul(out, lhsT, rhs, start=start, stop=stop, **kw)

            def chunk(c):
                pe.wait_ge(chunk_in[c % RING], 16 * (c // RING + 1))
                return c % RING

            def begin(n, before=None):
                pe.wait_ge(read[n % 2], n // 2 if before is None else before)
                return G[n % 2]

            def project(n, wslot, col, KT, rhs, before=None, start=0, cols=256, stop=True, width=T):
                out = begin(n, before) if start == 0 else G[n % 2]
                wide = min(512, width)
                for k in range(KT):
                    w = ring[:, wslot, k * cols + col:k * cols + col + P]
                    first, last = k == 0 and start == 0, k == KT - 1 and stop
                    m = mm(out[:, 0:wide], w, rhs(start + k)[:, 0:wide], first, last)
                    if width > 512:
                        m = mm(out[:, 512:width], w, rhs(start + k)[:, 512:width], first, last)
                if stop:
                    m.then_inc(tile_done, 1)

            def split_product(n, slot, p, KT, rhs, before=None, normed=None, start=0, stop=True):
                if start == 0:
                    begin(n, before)
                out = GF[n % 2]
                pe.wait_ge(split, p + 1)
                for k in range(KT):
                    if normed is not None:
                        pe.wait_ge(applied, normed + k)
                    for wpart, xpart in ((0, 0), (0, 1), (1, 0)):
                        w = ws[:, slot, wpart, k * P:(k + 1) * P]
                        for f in range(2):
                            fr = slice(f * HT, (f + 1) * HT)
                            m = mm(out[:, fr], w, rhs[:, xpart, start + k, fr],
                                   k == 0 and start == 0 and wpart + xpart == 0,
                                   stop and k == KT - 1 and wpart == 1)
                m.then_inc(tile_done if stop else half_used, 1)

            def rows(buf):
                return lambda k: buf[:, k, :]

            def stat(k, tiles, ones, width=T, src=None):
                if k == 0:
                    pe.wait_ge(stat_read, nstat[0])
                    for b in range(2):
                        pe.wait_ge(Q_read[b], nQ[b])
                    nstat[0] += 1
                if src is None:
                    pe.wait_ge(sq_ready, nready[0] + 1)
                    src = sq[:, nready[0] % 2, :]
                    nready[0] += 1
                wide = min(512, width)
                m = mm(QF[:, 0:wide], ones, src[:, 0:wide], k == 0, k == tiles - 1)
                if width > 512:
                    m = mm(QF[:, 512:width], ones, src[:, 512:width], k == 0, k == tiles - 1)
                m.then_inc(sq_used, 1)

            def fill_S(b):
                pe.wait_ge(S_read[b], nS[b])
                nS[b] += 1

            def fill_Q(b):
                pe.wait_ge(Q_read[b], nQ[b])
                nQ[b] += 1

            pe.wait_ge(const_in, 32)
            ones, ident = cst("ones"), cst("ident")

            def projections(name, tiles, KT, rhs, cols=256, after=None):
                for n in range(tiles):
                    if n % 2 == 0:
                        s = chunk(CHUNK[name] + n // 2)
                    project(TILE0[name] + n, s, n % 2 * P, KT, rhs, cols=cols)
                    if after:
                        after(n)

            def lagged_stat(n):
                if n:
                    stat(n - 1, KD, ones)

            def narrow(name, wname):
                out = begin(TILE0[name])
                o = PAR[wname][0]
                for k in range(KD):
                    w = par[:, o + k * NH:o + (k + 1) * NH]
                    mm(out[0:NH, 0:512], w, h[:, k, 0:512], k == 0, k == KD - 1)
                    m = mm(out[0:NH, 512:T], w, h[:, k, 512:T], k == 0, k == KD - 1)
                m.then_inc(tile_done, 1)

            def frame_major(n, lhs, sa, sc):
                out = begin(n)
                for k in range(KD):
                    mm(out[:, 0:256], lhs(k), ring[:, sa, k * 256:(k + 1) * 256], k == 0, k == KD - 1,
                       skip_group_check=True)
                    m = mm(out[:, 256:512], lhs(k), ring[:, sc, k * 256:(k + 1) * 256], False, k == KD - 1,
                           skip_group_check=True)
                m.then_inc(tile_done, 1)

            for k in range(KD):
                stat(k, KD, ones)
            pe.wait_ge(applied, APPLIED["mix0"])
            projections("glu", 8, KD, rows(h),
                        after=lambda n: n == 1 and [stat(k, KD, ones, MT) for k in range(KD)])
            for l in range(LAYERS):
                for n in range(4):
                    if n % 2 == 0:
                        s = chunk(CHUNK[f"mk{l}"] + n // 2)
                    project(TILE0[f"mk{l}"] + n, s, n % 2 * P, KD, lambda k, l=l: memh[:, l, k, :], width=MT)
                    if n:
                        stat(0, 1, ones, MT)
                stat(0, 1, ones, MT)
                sa, sc = chunk(CHUNK[f"mv{l}"]), chunk(CHUNK[f"mv{l}"] + 1)
                for m2 in range(2):
                    frame_major(TILE0[f"mv{l}"] + m2, lambda k: memh[:, l, k, m2 * P:(m2 + 1) * P], sa, sc)
            projections("xbc", 8, KD, rows(h))
            narrow("dt", "wdt")
            projections("z", 4, KD, rows(h))
            pe.wait_ge(conv, 8 * CW)
            for k in range(4):
                stat(k, 4, ones, src=acc[:, k, :])
            n = TILE0["tok"]
            out = begin(n)
            pe.wait_ge(de_ready, 1)
            for v in range(2):
                for c in range(NCH):
                    at = (v * NCH + c) * NH
                    m = nc.tensor.transpose(out[:, at:at + NH], dtb[:, 1 + v, c * P:(c + 1) * P],
                                            ident[0:NH, 0:NH])
            m.then_inc(tile_done, 1)
            out = begin(n + 1)
            mm(out[:, 0:NSEG * NH], ones[0:NH, :], cdiag[:, :, :].rearrange("p a b -> p (a b)"), True, True)\
                .then_inc(tile_done, 1)
            for k in range(4):
                stat(k, 4, ones)
            n = TILE0["scan"]
            d8, sel = cst("d8", NH), cst("sel", NH)
            pe.wait_ge(xbc_done, KD)
            for c in range(NCH):
                fr = slice(c * P, (c + 1) * P)
                run = c == NCH - 1
                out = begin(n)
                for j in range(4):
                    m = nc.tensor.transpose(out[:, j * P:(j + 1) * P], xbcc[:, j, fr], ident)
                m.then_inc(tile_done, 1)
                out = begin(n + 1)
                for j in range(2):
                    m = nc.tensor.transpose(out[:, j * P:(j + 1) * P], xbcc[:, 4 + j, fr], ident)
                m.then_inc(tile_done, 1)
                if c == 0:
                    pe.wait_ge(stat_read, nstat[0])
                fill_Q(0)
                for gr in range(2):
                    m = mm(Q[:, 0, gr * P:(gr + 1) * P], xbcc[:, 4 + gr, fr], xbcc[:, 6 + gr, fr], True, True)
                m.then_inc(Q_done, 1)
                mask = cst("smask" if run else "lmask")
                for gr in range(2):
                    fill_S(gr)
                    o = S[:, gr, :].rearrange("p (h l) -> p h l", h=4)
                    mm(o, ident, mask.unsqueeze(1).broadcast_to([P, 4, P]), True, False, skip_group_check=True)
                    mm(o, dtb[:, 0, fr], d8[:, 4 * gr:4 * gr + 4].unsqueeze(2).broadcast_to([NH, 4, P]),
                       False, False, skip_group_check=True)
                    for hh in range(4):
                        m = mm(o[:, hh, :], d8[:, 4 * gr + hh:4 * gr + hh + 1].broadcast_to([NH, P]),
                               dtb[:, 3, fr], False, hh == 3, skip_group_check=True)
                    m.then_inc(S_done, 1)
                fill_Q(1)
                for j in range(4):
                    m = mm(Q[:, 1, j * P:(j + 1) * P],
                           sel[:, j * P:(j + 1) * P], dtb[:, 3, fr], True, True)
                m.then_inc(Q_done, 1)
                out = begin(n + 2)
                read_wait(pe, n)
                pe.wait_ge(Q_read[0], nQ[0])
                for hh in range(NH):
                    e = hh % 2
                    m = mm(out[64 * e:64 * e + 64, hh // 2 * P:(hh // 2 + 1) * P],
                           xdt[:, hh * HD:(hh + 1) * HD], Pm[:, hh, :], True, True, skip_group_check=True)
                m.then_inc(tile_done, 1)
                out = begin(n + 3)
                if run:
                    pe.wait_ge(state_in, 16)
                    for rq in range(REQ):
                        for j in range(4):
                            at = SEQ + rq * STEP
                            m = mm(out[:, j * P + rq * STEP:j * P + (rq + 1) * STEP],
                                   h0T[:, rq, j * P:(j + 1) * P], xbcc[:, 6 + j // 2, at:at + STEP], True, True)
                else:
                    if c == 0:
                        pe.wait_ge(hT_zero, 1)
                    else:
                        read_wait(pe, n - 1)
                    for j in range(4):
                        m = mm(out[:, j * P:(j + 1) * P], hT[:, j * P:(j + 1) * P], xbcc[:, 6 + j // 2, fr],
                               True, True)
                m.then_inc(tile_done, 1)
                pe.wait_ge(xdte_ready, c + 1)
                read_wait(pe, n + 1)
                for k in range(REQ if run else 1):
                    out = begin(n + 4 + k)
                    for gr in range(2):
                        b = bmask[:, k, gr * P:(gr + 1) * P] if run else btok[:, gr * P:(gr + 1) * P]
                        m = mm(out[:, gr * 256:(gr + 1) * 256], b, xdte[:, gr * 256:(gr + 1) * 256], True, True)
                    m.then_inc(tile_done, 1)
                n += 5
            for gr in range(2):
                for k in range(2):
                    stat(k, 2, ones)

            def cross_and_ffn(l):
                stat(KD - 1, KD, ones)
                pe.wait_ge(applied, APPLIED[f"cross{l}"])
                projections(f"q{l}", 4, KD, rows(h), after=lambda n: n and stat(0, 1, ones))
                stat(0, 1, ones)
                pe.wait_ge(applied, APPLIED[f"q{l}.3"])
                pe.wait_ge(stat_read, nstat[0])

                def scores(it):
                    b = it % 2
                    fill_S(b)
                    if it >= 8:
                        pe.wait_ge(qblk_ready, 1 if l == 0 else 2 + REQ)
                    for sl in range(2):
                        o = S[:, b, sl * MT:(sl + 1) * MT]
                        if it < 8:
                            qt, hh = it // 2, 2 * (it % 2) + sl
                            m = mm(o, xq[:, hh, qt * P:(qt + 1) * P], mkT[:, l, hh, :], True, True)
                            continue
                        pair = 2 * (it - 8) + sl
                        pe.wait_ge(xcache_in[pair], 32 * (l + 1))
                        for e in range(2):
                            for hh in range(MH):
                                m = mm(o[64 * e:64 * e + 64, :], xqb[:, 2 * pair + e, hh * 64:(hh + 1) * 64],
                                       xkc[:, pair, e, hh, :], hh == 0, hh == MH - 1)
                    m.then_inc(S_done, 1)

                def transposes(it):
                    b = it % 2
                    fill_Q(b)
                    pe.wait_ge(prob_ready, (NX + NFOX) * l + it + 1)
                    for k in range(4):
                        m = nc.tensor.transpose(Q[:, b, k * P:(k + 1) * P],
                                                xP[:, b, k // 2, k % 2 * P:(k % 2 + 1) * P], ident)
                    m.then_inc(Q_done, 1)

                def values(it):
                    b = it % 2
                    out = begin(TILE0[f"xo{l}"] + it)
                    pe.wait_ge(Q_read[b], nQ[b])
                    for sl in range(2):
                        if it < 8:
                            hh = 2 * (it % 2) + sl
                            for kh in range(2):
                                m = mm(out[:, sl * P:(sl + 1) * P], mv[:, l, kh, hh * P:(hh + 1) * P],
                                       xPT[:, b, 2 * sl + kh, :], kh == 0, kh == 1)
                            continue
                        pair = 2 * (it - 8) + sl
                        for e in range(2):
                            for hh in range(MH):
                                at = e * 64 + hh * STEP
                                for kh in range(2):
                                    m = mm(out[:, sl * P + at:sl * P + at + STEP],
                                           xvc[:, pair, e, kh, hh * P:(hh + 1) * P],
                                           xPT[:, b, 2 * sl + kh, at:at + STEP], kh == 0, kh == 1)
                    m.then_inc(tile_done, 1)

                for it in range(NX + 2):
                    if it < NX:
                        scores(it)
                    if 1 <= it <= NX:
                        transposes(it - 1)
                    if it >= 2:
                        values(it - 2)
                read_wait(pe, TILE0[f"xo{l}"] + NX - 2)
                read_wait(pe, TILE0[f"xo{l}"] + NX - 1)
                projections(f"wo{l}", 8, 4, rows(xo), after=lagged_stat)
                stat(KD - 1, KD, ones)
                for half in "ab":
                    t0, p0 = TILE0[f"up{l}{half}"], PIECE0[f"up{l}{half}"]
                    first = APPLIED[f"ffn{l}"] - KD + 1 if half == "a" else None
                    for j in range(2):
                        split_product(t0 + j, j, p0 + j, KD, hs, normed=first if j == 0 else None)
                    with pe.Fori(1, HALF) as i:
                        for j in range(2):
                            split_product(t0 + j, j, i * 2 + (p0 + j), KD, hs, before=i + (t0 + j) // 2)
                    t0, p0 = TILE0[f"down{l}{half}"], PIECE0[f"down{l}{half}"]
                    read_wait(pe, t0 - 1)
                    with pe.Fori(0, KD // 2) as i:
                        for j in range(2):
                            n, p = t0 + j, i * 4 + (p0 + 2 * j)
                            split_product(n, 0, p, KS, gs, before=i + n // 2, stop=False)
                            split_product(n, 1, p + 1, HALF - KS, gs, start=KS)

            pe.wait_ge(mixed, 4)
            pe.wait_ge(applied, APPLIED["gn1"])
            projections("evout", 8, KD, rows(h), after=lagged_stat)
            cross_and_ffn(0)
            for k in range(KD):
                stat(k, KD, ones)
            pe.wait_ge(applied, APPLIED["mix1"])
            projections("cgu", 8, KD, rows(h))
            narrow("f", "wf")
            projections("gb", 4, KD, rows(h))
            projections("fqk", 8, KD, rows(h), after=lambda n: n and stat(0, 1, cst("half")))
            stat(0, 1, cst("half"))
            sa, sc = chunk(CHUNK["fv"]), chunk(CHUNK["fv"] + 1)
            for c in range(NCH):
                frame_major(TILE0["fv"] + c, lambda k: h[:, k, c * P:(c + 1) * P], sa, sc)
            pe.wait_ge(applied, APPLIED["fqk.7"])
            read_wait(pe, TILE0["fv"] + NCH - 2)
            read_wait(pe, TILE0["fv"] + NCH - 1)
            pe.wait_ge(fcum_ready, 1)
            pe.wait_ge(stat_read, nstat[0])
            d8, nd8 = cst("d8", NH), cst("nd8", NH)
            nd16 = cst("nd16", NH)

            def fox_scores(it):
                b = it % 2
                fill_S(b)
                if it < 4 * NH:
                    hh, qt = FOX_ITEMS[it]
                    e, j, w = hh % 2, hh // 2, (qt + 1) * P
                    o, fr = S[:, b, 0:w], slice(qt * P, (qt + 1) * P)
                    mm(o, fqk[64 * e:64 * e + 64, j, fr], fqk[64 * e:64 * e + 64, 4 + j, 0:w], True, False,
                       skip_group_check=True)
                    mm(o, fcp[:, fr], d8[:, hh:hh + 1].broadcast_to([NH, w]), False, False,
                       skip_group_check=True)
                    mm(o, nd8[:, hh:hh + 1].broadcast_to([NH, P]), fcp[:, 0:w], False, False,
                       skip_group_check=True)
                    m = mm(S[:, b, qt * P:w], ident, cst("cmask"), False, True, skip_group_check=True)
                else:
                    rq = it - 4 * NH
                    old, new = S[:, b, 0:PAST], S[:, b, PAST:PAST + P]
                    pe.wait_ge(qblk_ready, 1 + rq + 1)
                    pe.wait_ge(keys_in[rq % 2], 16 * (rq // 2 + 1))
                    for j in range(4):
                        w = qblk[:, rq % 2, j * P:(j + 1) * P]
                        mm(old, w, kc[:, rq % 2, j, :], j == 0, False, skip_group_check=True)
                        mm(new, w, fqk[:, 4 + j, SEQ:T], False, False, skip_group_check=True)
                    mm(S[:, b, 0:384], fqd[:, rq % 2, :, :].rearrange("p a b -> p (a b)"),
                       ones[0:NH, 0:1].broadcast_to([NH, 384]), False, False, skip_group_check=True)
                    mm(old, nd16, fcr[:, rq, 0:PAST], False, False, skip_group_check=True)
                    mm(new, nd16, fcr[:, :, PAST:KALL], False, False, skip_group_check=True)
                    o = CONST["negwin"][0] + (REQ - 1 - rq) * STEP
                    mm(new, ones[0:1, :], const[0:1, o:o + P], False, False, skip_group_check=True)
                    m = mm(new[:, rq * STEP:(rq + 1) * STEP], cst("r16", STEP), cst("m16", STEP), False, True,
                           skip_group_check=True)
                m.then_inc(S_done, 1)

            def fox_tiles(it):
                return FOX_ITEMS[it][1] + 1 if it < 4 * NH else 3

            def fox_transposes(it):
                b = it % 2
                fill_Q(b)
                pe.wait_ge(prob_ready, NX + it + 1)
                for k in range(fox_tiles(it)):
                    m = nc.tensor.transpose(Q[:, b, k * P:(k + 1) * P], fP[:, b, k * P:(k + 1) * P], ident)
                m.then_inc(Q_done, 1)

            def fox_values(it):
                b = it % 2
                out = begin(TILE0["fo"] + it)
                pe.wait_ge(Q_read[b], nQ[b])
                kt = fox_tiles(it)
                if it < 4 * NH:
                    hh = FOX_ITEMS[it][0]
                    e = hh % 2
                    for k in range(kt):
                        m = mm(out[64 * e:64 * e + 64, 0:P], fv[:, k, hh * HD:(hh + 1) * HD], fPT[:, b, k, :],
                               k == 0, k == kt - 1)
                else:
                    rq = it - 4 * NH
                    pe.wait_ge(values_in[rq % 2], 16 * (rq // 2 + 1))
                    for j in range(4):
                        for k in range(kt):
                            v = vc[:, rq % 2, k, j * P:(j + 1) * P] if k < 2 else fv[:, 4, j * P:(j + 1) * P]
                            m = mm(out[:, j * 32:(j + 1) * 32], v, fPT[:, b, k, j * 32:(j + 1) * 32],
                                   k == 0, k == kt - 1)
                m.then_inc(tile_done, 1)

            for it in range(NFOX + 2):
                if it < NFOX:
                    fox_scores(it)
                if 1 <= it <= NFOX:
                    fox_transposes(it - 1)
                if it >= 2:
                    fox_values(it - 2)
            read_wait(pe, TILE0["fo"] + NFOX - 2)
            read_wait(pe, TILE0["fo"] + NFOX - 1)
            projections("odout", 8, KD, lambda k: (cacc if k < 4 else h)[:, k, :], after=lagged_stat)
            cross_and_ffn(1)

        @block.scalar
        def _(act):
            nsq, nsum, nstat, nself = [0], [0], [0], [0]

            def A(*a, **k):
                return nc.scalar.activation(*a, **k)

            def own(ins):
                ins.then_inc(act_self, 1)
                nself[0] += 1
                act.wait_ge(act_self, nself[0])

            def square(src, width=T):
                if nsq[0] >= 2:
                    act.wait_ge(sq_used, summed(nsq[0] - 2))
                A(sq[:, nsq[0] % 2, 0:width], src, ACT.Square).then_inc(sq_ready, 1)
                nsq[0] += 1

            def sums(tiles):
                nsum[0] += tiles
                act.wait_ge(sq_used, nsum[0])
                m = nstat[0]
                if m >= 2:
                    by_pool, count = NORM[m - 2]
                    act.wait_ge(mk_applied if by_pool else applied, count)
                nstat[0] += 1
                return rstd[:, m % 2, :]

            def inv_std(tiles, scale, eps=0, width=T):
                r = sums(tiles)[:, 0:width]
                A(r, QF[:, 0:width], ACT.Ln, scale=scale, bias=small[:, eps:eps + 1]).then_inc(stat_read, 1)
                act.wait_ge(stat_read, nstat[0])
                A(r, r, ACT.Exp, scale=-0.5).then_inc(rstd_ready, 1)

            def evacuate(dst, n, func=ACT.Copy, width=T):
                tile_wait(act, n)
                A(dst, G[n % 2][:, 0:width], func).then_inc(read[n % 2], 1)

            def head_norms(dst, n0, tiles, scale, width=T):
                for j in range(tiles):
                    evacuate(dst(j), n0 + j, width=width)
                    read_wait(act, n0 + j)
                    square(dst(j), width)
                    if j:
                        inv_std(1, scale, width=width)
                inv_std(1, scale, width=width)

            def high_part(name, u, s, done, count, i=0):
                c = CHUNK[name] + u
                if s == 0:
                    act.wait_ge(chunk_in[c % RING], i * 16 + 16 * (c // RING + 1))
                act.wait_ge(done, count)
                src, hi, _ = piece(name, u, s)
                A(hi, src, ACT.Copy).then_inc(high, 1)

            def residual_squares(name, after=None):
                for j in range(KD):
                    read_wait(act, TILE0[name] + j)
                    square(x[:, j, :])
                    if after:
                        after(j)
                inv_std(KD, 1.0 / D)

            act.wait_ge(x_in, 16)
            act.wait_ge(small_ready, 1)
            for k in range(KD):
                square(x[:, k, :])
            inv_std(KD, 1.0 / D)
            t0 = TILE0["glu"]
            for j in range(4):
                if j >= 2:
                    read_wait(act, t0 + 2 * (j - 2) + 1)
                evacuate(tmp[:, j % 2, :], t0 + 2 * j, ACT.Sigmoid)
                if j == 0:
                    act.wait_ge(mem_in, 16)
                    for k in range(KD):
                        square(memx[:, k, :], MT)
                    inv_std(KD, 1.0 / D, width=MT)
            for l in range(LAYERS):
                head_norms(lambda j: mkT[:, l, j, :], TILE0[f"mk{l}"], 4, 1.0 / P, MT)
                for m2 in range(2):
                    evacuate(mv[:, l, m2, :], TILE0[f"mv{l}"] + m2, width=512)
            act.wait_ge(const_in, 32)
            for j in range(KD):
                n = TILE0["xbc"] + j
                tile_wait(act, n)
                a, b = padded(xbcp, j, XW - 1, XPROMPT, XREQ, XW - 1)
                A(a, G[n % 2][:, 0:SEQ], ACT.Copy)
                A(b, runs(G[n % 2][:, SEQ:T]), ACT.Copy).then_inc(read[n % 2], 1)
            for j in range(KD):
                act.wait_ge(xconv, 2 * XW * (j + 1))
                A(xbcc[:, j, :], tmp[:, j % 2, :], ACT.Silu).then_inc(xbc_done, 1)
            act.wait_ge(dt_abs, 1)
            own(A(dtb[:, 2, :], dtb[:, 2, :], ACT.Exp, scale=-1.0))
            A(small[0:NH, 3:4], pr("alog", 0, NH), ACT.Exp)
            A(dtb[:, 2, :], dtb[:, 2, :], ACT.Ln, bias=small[0:NH, 2:3]).then_inc(dt_log, 1)
            act.wait_ge(applied, APPLIED["mem"])
            for j in range(4):
                evacuate(zs[:, j, :], TILE0["z"] + j, ACT.Silu)
            r = sums(4)
            A(r, QF[:, 0:T], ACT.Copy).then_inc(stat_read, 1)
            act.wait_ge(stat_read, nstat[0])
            A(r, r, ACT.Copy, scale=1.0 / CONF).then_inc(rstd_ready, 1)
            act.wait_ge(cs_ready, 1)
            A(dtb[:, 2, :], dtb[:, 2, :], ACT.Exp, scale=-1.0).then_inc(de_ready, 1)
            n = TILE0["tok"] + 1
            tile_wait(act, n)
            A(decay[:, :, :].rearrange("p a b -> p (a b)"), G[n % 2][:, 0:NSEG * NH], ACT.Exp)\
                .then_inc(read[n % 2], 1)
            act.wait_ge(applied, APPLIED["mean"])
            for k in range(4):
                square(acc[:, k, :])
            inv_std(4, 1.0 / CONF, eps=1)
            act.wait_ge(applied, APPLIED["var"])
            for k in range(4):
                A(h[:, k, :], acc[:, k, :], ACT.Silu, scale=pr("lng", k), bias=pr("lnb", k)).then_inc(mixed, 1)
            act.wait_ge(outs, 16 * CONV_OUTS)
            n = TILE0["scan"]
            for c in range(NCH):
                if c < NCH - 1:
                    tile_wait(act, n + 1)
                    A(btok, G[(n + 1) % 2][:, 0:256], ACT.Copy).then_inc(read[(n + 1) % 2], 1)
                act.wait_ge(Q_read[0], c)
                for gr in range(2):
                    act.wait_ge(S_done, 2 * c + gr + 1)
                    A(Lm[:, 4 * gr:4 * gr + 4, :].rearrange("p a b -> p (a b)"), S[:, gr, :], ACT.Exp)\
                        .then_inc(S_read[gr], 1)
                if c:
                    read_wait(act, n - 2)
                elif c == 0:
                    act.wait_ge(mixed, 4)
                act.wait_ge(Q_done, 2 * c + 2)
                A(Ee.rearrange("p a b -> p (a b)"), Q[:, 1, :], ACT.Exp).then_inc(Q_read[1], 1)
                n += 5
            act.wait_ge(gated, NCH)
            for gr in range(2):
                for k in range(2):
                    square(h[:, 4 + 2 * gr + k, :])
                inv_std(2, 1.0 / 256)

            def cross_and_ffn(l):
                act.wait_ge(outs, 16 * (ODD_OUTS if l else SCAN_OUTS))
                head_norms(lambda j: xq[:, j, :], TILE0[f"q{l}"], 4, 1.0 / P)
                first = (NX + NFOX) * l

                def exps(it):
                    b, i = it % 2, first + it
                    act.wait_ge(neg_ready, i + 1)
                    act.wait_ge(Q_done, 2 * NCH + i - 1)
                    for sl in range(2):
                        m = A(xP[:, b, sl, :], S[:, b, sl * MT:(sl + 1) * MT], ACT.Exp, scale=SCALE_X,
                              bias=stats[:, b, 2 + sl:3 + sl], accum_out=stats[:, b, 4 + sl:5 + sl])
                    m.then_inc(S_read[b], 1)

                def turned(it):
                    b, i = it % 2, first + it
                    act.wait_ge(Q_done, 2 * NCH + i + 1)
                    if it >= 2:
                        tile_wait(act, TILE0[f"xo{l}"] + it - 2)
                    A(xPT[:, b, :, :].rearrange("p a b -> p (a b)"), Q[:, b, :], ACT.Copy)\
                        .then_inc(Q_read[b], 1)

                for it in range(NX + 1):
                    if it < NX:
                        exps(it)
                    if it:
                        turned(it - 1)
                residual_squares(f"wo{l}", lambda j: j == 5 and [
                    high_part(f"up{l}a", 0, s, tile_done, TILE0[f"wo{l}"] + 1) for s in range(2)])
                for k in range(KD):
                    act.wait_ge(h_raw, KD * l + k + 1)
                    A(hs[:, 0, k, :], raw_tile(k), ACT.Copy).then_inc(h_hi, 1)

                def gate(j, n, step=0):
                    act.wait_ge(read[(n + 1) % 2], step * RING + (n - 3) // 2 + 1)
                    act.wait_ge(tile_done, step * (2 * RING) + n + 1)
                    A(tmp[:, j % 2, :], GF[n % 2], ACT.Silu).then_inc(read[n % 2], 1)

                for half in "ab":
                    up, down = f"up{l}{half}", f"down{l}{half}"
                    t0 = TILE0[up]

                    def tiles(u, i=0):
                        for s in range(2):
                            n = t0 + 2 * u + s
                            if s == 0:
                                gate(u, n, i)
                            nxt = (up, u + 1) if u < HALF - 1 else (down, 0)
                            high_part(*nxt, s, tile_done, i * (2 * RING) + n + 1, i)

                    with act.Fori(0, HALF // RING) as i:
                        for u in range(RING):
                            tiles(u, i)
                    for u in range(HALF // RING * RING, HALF):
                        tiles(u)
                    for j in range(KD):
                        nxt = (down, j + 1) if j < KD - 1 else (f"up{l}b", 0)
                        if j < KD - 1 or half == "a":
                            high_part(*nxt, 0, half_used, KD * (2 * l + (half == "b")) + j + 1)
                            high_part(*nxt, 1, tile_done, TILE0[down] + j + 1)

            residual_squares("evout")
            cross_and_ffn(0)
            residual_squares("down0b")
            t0 = TILE0["cgu"]
            for j in range(4):
                if j >= 2:
                    read_wait(act, t0 + 2 * (j - 2) + 1)
                evacuate(tmp[:, j % 2, :], t0 + 2 * j)
            act.wait_ge(f_abs, 1)
            own(A(tmp[0:NH, 1, :], tmp[0:NH, 1, :], ACT.Exp, scale=-1.0))
            A(tmp[0:NH, 1, :], tmp[0:NH, 1, :], ACT.Ln, bias=small[0:NH, 2:3]).then_inc(f_log, 1)
            head_norms(lambda j: fqk[:, j, :], TILE0["fqk"], 8, 1.0 / HD)
            for c in range(NCH):
                evacuate(fv[:, c, :], TILE0["fv"] + c, width=512)

            def fox_width(it):
                return (FOX_ITEMS[it][1] + 1) * P if it < 4 * NH else 384

            def fox_exps(it):
                b, i, w = it % 2, NX + it, fox_width(it)
                act.wait_ge(neg_ready, i + 1)
                act.wait_ge(Q_done, 2 * NCH + i - 1)
                A(fP[:, b, 0:w], S[:, b, 0:w], ACT.Exp, bias=stats[:, b, 2:3],
                  accum_out=stats[:, b, 4:5]).then_inc(S_read[b], 1)

            def fox_turned(it):
                b, i, w = it % 2, NX + it, fox_width(it)
                act.wait_ge(Q_done, 2 * NCH + i + 1)
                if it >= 2:
                    tile_wait(act, TILE0["fo"] + it - 2)
                A(fPT[:, b, :, :].rearrange("p a b -> p (a b)")[:, 0:w], Q[:, b, 0:w], ACT.Copy)\
                    .then_inc(Q_read[b], 1)

            for it in range(NFOX + 1):
                if it < NFOX:
                    fox_exps(it)
                if it:
                    fox_turned(it - 1)
            residual_squares("odout")
            cross_and_ffn(1)

        @block.vector
        def _(dve):
            v = nc.vector
            nself, nnorm = [0], [0]

            def own(ins):
                ins.then_inc(dve_self, 1)
                nself[0] += 1
                dve.wait_ge(dve_self, nself[0])

            def norm(pairs, gain, width=T):
                m = nnorm[0]
                dve.wait_ge(rstd_ready, m + 1)
                for j, (dst, src) in enumerate(pairs):
                    v.scalar_tensor_tensor(out=dst, in0=src, scalar=gain(j), in1=rstd[:, m % 2, 0:width],
                                           op0=ALU.mult, op1=ALU.mult).then_inc(applied, 1)
                nnorm[0] += 1

            def norm_x(name):
                norm([(h[:, k, :], x[:, k, :]) for k in range(KD)], lambda k: pr(name, k))

            def add_residual(name, after=None):
                for j in range(KD):
                    n = TILE0[name] + j
                    tile_wait(dve, n)
                    v.tensor_tensor(x[:, j, :], x[:, j, :], G[n % 2][:, 0:T], ALU.add)\
                        .then_inc(read[n % 2], 1)
                    if after:
                        after(j)

            def low_part(name, u, s, i=0):
                dve.wait_ge(high, i * (2 * RING) + (PIECE0[name] + 2 * u + s + 1))
                src, hi, lo = piece(name, u, s)
                v.tensor_tensor(lo, src, hi.bitcast(F32), ALU.subtract).then_inc(split, 1)

            v.memset(small[:, 0:1], 1e-6)
            v.memset(small[:, 1:2], 1e-5)
            v.memset(small[:, 2:3], 1.0).then_inc(small_ready, 1)
            v.memset(aglu[:, :, 0:CW - 1], 0.0)
            v.memset(xbcp[:, :, 0:XW - 1], 0.0).then_inc(small_ready, 1)
            v.memset(hT, 0.0).then_inc(hT_zero, 1)
            dve.wait_ge(const_in, 32)
            dve.wait_ge(x_in, 16)
            v.tensor_scalar(small[:, 4:5], pr("fq"), HD ** -0.5, None, ALU.mult)
            norm_x("mix0")
            for j in range(4):
                n = TILE0["glu"] + 2 * j
                read_wait(dve, n)
                tile_wait(dve, n + 1)
                a, b = padded(aglu, j, CW - 1, CPROMPT, CREQ, CW - 1)
                v.tensor_tensor(a, tmp[:, j % 2, 0:SEQ], G[(n + 1) % 2][:, 0:SEQ], ALU.mult)
                v.tensor_tensor(b, runs(tmp[:, j % 2, SEQ:T]), runs(G[(n + 1) % 2][:, SEQ:T]), ALU.mult)\
                    .then_inc(read[(n + 1) % 2], 1)
                if j == 0:
                    norm([(memh[:, l, k, :], memx[:, k, :]) for l in range(2) for k in range(KD)],
                         lambda i: pr(f"mem{i // KD}", i % KD), MT)
            nnorm[0] += 8
            dve.wait_ge(pads_in, 16 * 12)
            dve.wait_ge(small_ready, 2)
            read_wait(dve, TILE0["glu"] + 5)
            read_wait(dve, TILE0["glu"] + 7)
            dst = [d for j in range(4) for d in (acc[:, j, 0:SEQ], runs(acc[:, j, SEQ:T]))]
            for i, d in enumerate(dst):
                src = padded(aglu, i // 2, 0, CPROMPT, CREQ, 0)[i % 2]
                v.tensor_scalar(d, src, pr("cw", i // 2 * CW), pr("cb", i // 2), ALU.mult, ALU.add)\
                    .then_inc(conv, 1)
            with dve.Fori(1, CW) as w:
                for i, d in enumerate(dst):
                    j = i // 2
                    if i % 2 == 0:
                        src = aglu[:, j, bass.ds(w, SEQ)]
                    else:
                        src = aglu[:, j, CPROMPT:].rearrange("p (r t) -> p r t", r=REQ)[:, :, bass.ds(w, STEP)]
                    tap = par[:, bass.ds(w + (PAR["cw"][0] + j * CW), 1)]
                    dve.wait_ge(conv, w * 8 + (i - 7))
                    v.scalar_tensor_tensor(out=d, in0=src, scalar=tap, in1=d, op0=ALU.mult, op1=ALU.add)\
                        .then_inc(conv, 1)
            done = 0
            for j in range(KD):
                read_wait(dve, TILE0["xbc"] + j)
                if j >= 2:
                    dve.wait_ge(xbc_done, j - 1)
                out = (tmp[:, j % 2, 0:SEQ], runs(tmp[:, j % 2, SEQ:T]))
                for w in range(XW):
                    for i in range(2):
                        src = padded(xbcp, j, 0, XPROMPT, XREQ, w)[i]
                        if w == 0:
                            ins = v.tensor_scalar(out[i], src, pr("xw", j * XW), pr("xb", j), ALU.mult, ALU.add)
                        else:
                            dve.wait_ge(xconv, done - 1)
                            ins = v.scalar_tensor_tensor(out=out[i], in0=src, scalar=pr("xw", j * XW + w),
                                                         in1=out[i], op0=ALU.mult, op1=ALU.add)
                        ins.then_inc(xconv, 1)
                        done += 1
            n = TILE0["dt"]
            tile_wait(dve, n)
            v.tensor_scalar(dtb[:, 1, :], G[n % 2][0:NH, 0:T], pr("dtb", 0, NH), None, ALU.add)\
                .then_inc(read[n % 2], 1)
            read_wait(dve, n)
            v.scalar_tensor_tensor(out=dtb[:, 2, :], in0=dtb[:, 1, :], scalar=-1.0, in1=dtb[:, 1, :],
                                   op0=ALU.mult, op1=ALU.max).then_inc(dt_abs, 1)
            dve.wait_ge(dt_log, 1)
            own(v.scalar_tensor_tensor(out=dtb[:, 1, :], in0=dtb[:, 1, :], scalar=0.0, in1=dtb[:, 2, :],
                                       op0=ALU.max, op1=ALU.add))
            own(v.tensor_scalar(dtb[:, 0, :], dtb[:, 1, :], small[0:NH, 3:4], -1.0, ALU.mult, ALU.mult))
            segments = [(c * P, P) for c in range(4)] + [(SEQ + q * STEP, STEP) for q in range(REQ)]
            one = cst("ones", NH)[:, 0:1]
            for at, w in segments:
                ins = v.tensor_tensor_scan(out=dtb[:, 3, at:at + w], data0=one.broadcast_to([NH, w]), data1=dtb[:, 0, at:at + w],
                                           initial=0.0, op0=ALU.mult, op1=ALU.add)
            own(ins)
            v.tensor_scalar(dtb[:, 0, :], dtb[:, 3, :], -1.0, None, ALU.mult)
            v.tensor_copy(csend[:, 0:4], dtb[:, 3, P - 1:SEQ:P])
            own(v.tensor_copy(csend[:, 4:NSEG], dtb[:, 3, SEQ + STEP - 1:T:STEP]))
            v.tensor_tensor(cdiag[:, :, :], csend[:, :].unsqueeze(2).broadcast_to([NH, NSEG, NH]),
                            cst("d8", NH).unsqueeze(1).broadcast_to([NH, NSEG, NH]), ALU.mult)
            for at, w, s0, ns in ((0, P, 0, 4), (SEQ, STEP, 4, REQ)):
                seg = lambda row: dtb[:, row, at:at + w * ns].rearrange("p (s t) -> p s t", s=ns)
                ins = v.tensor_tensor(seg(2), seg(3), csend[:, s0:s0 + ns].unsqueeze(2).broadcast_to([NH, ns, w]),
                                      ALU.subtract)
            ins.then_inc(cs_ready, 1)
            m = nnorm[0]
            dve.wait_ge(rstd_ready, m + 1)
            for k in range(4):
                v.tensor_tensor(acc[:, k, :], acc[:, k, :], rstd[:, m % 2, :], ALU.subtract).then_inc(applied, 1)
            n = TILE0["tok"]
            tile_wait(dve, n)
            v.tensor_copy(toks[:, :, :, :].rearrange("p a b c -> p (a b c)"), G[n % 2][:, 0:2 * NCH * NH])\
                .then_inc(read[n % 2], 1)
            dve.wait_ge(rstd_ready, m + 2)
            for k in range(4):
                v.tensor_tensor(acc[:, k, :], acc[:, k, :], rstd[:, (m + 1) % 2, :], ALU.mult).then_inc(applied, 1)
            nnorm[0] += 2
            read_wait(dve, n)
            read_wait(dve, n + 1)
            dve.wait_ge(outs, 16 * CONV_OUTS)
            n = TILE0["scan"]
            for c in range(NCH):
                fr = slice(c * P, (c + 1) * P)
                run = c == NCH - 1
                heads = lambda ap: ap.rearrange("p (h d) -> p h d", d=HD)
                tile_wait(dve, n)
                v.tensor_tensor(heads(xdt), heads(G[n % 2][:, 0:512]),
                                toks[:, 0, c, :].unsqueeze(2).broadcast_to([P, NH, HD]), ALU.mult)\
                    .then_inc(read[n % 2], 1)
                read_wait(dve, n)
                v.tensor_tensor(heads(xdte), heads(xdt), toks[:, 1, c, :].unsqueeze(2).broadcast_to([P, NH, HD]),
                                ALU.mult).then_inc(xdte_ready, 1)
                if run:
                    tile_wait(dve, n + 1)
                    v.tensor_tensor(bmask, G[(n + 1) % 2][:, 0:256].unsqueeze(1).broadcast_to([P, REQ, 256]),
                                    cst("req").unsqueeze(2).broadcast_to([P, REQ, 256]), ALU.mult)\
                        .then_inc(read[(n + 1) % 2], 1)
                dve.wait_ge(Q_done, 2 * c + 1)
                if c == 0:
                    dve.wait_ge(mixed, 4)
                for gr in range(2):
                    dve.wait_ge(S_read[gr], c + 1)
                    ins = v.tensor_tensor(Pm[:, 4 * gr:4 * gr + 4, :], Lm[:, 4 * gr:4 * gr + 4, :],
                                          Q[:, 0, gr * P:(gr + 1) * P].unsqueeze(1).broadcast_to([P, 4, P]),
                                          ALU.mult)
                ins.then_inc(Q_read[0], 1)
                tile_wait(dve, n + 3)
                dve.wait_ge(Q_read[1], c + 1)
                four = lambda n: G[n % 2][:, 0:512].rearrange("p (j l) -> p j l", j=4)
                v.tensor_tensor(ysc, four(n + 3), Ee, ALU.mult).then_inc(read[(n + 3) % 2], 1)
                read_wait(dve, n + 3)
                v.tensor_tensor(ysc, ysc, four(n + 2), ALU.add).then_inc(read[(n + 2) % 2], 1)
                if run:
                    own(v.tensor_tensor(h0T.rearrange("p r (h d) -> p (r h) d", d=HD),
                                        h0T.rearrange("p r (h d) -> p (r h) d", d=HD),
                                        decay[:, 4:NSEG, :].rearrange("p r h -> p (r h)").unsqueeze(2)
                                        .broadcast_to([P, REQ * NH, HD]), ALU.mult))
                else:
                    own(v.tensor_tensor(heads(hT), heads(hT),
                                        decay[:, c, :].unsqueeze(2).broadcast_to([P, NH, HD]), ALU.mult))
                for k in range(REQ if run else 1):
                    tile_wait(dve, n + 4 + k)
                    st = h0T[:, k, :] if run else hT
                    v.tensor_tensor(st, st, G[(n + 4 + k) % 2][:, 0:512], ALU.add)\
                        .then_inc(read[(n + 4 + k) % 2], 1)
                read_wait(dve, n + 2)
                for j in range(4):
                    ins = v.scalar_tensor_tensor(out=h[:, 4 + j, fr], in0=xbcc[:, j, fr], scalar=pr("dskip", j),
                                                 in1=ysc[:, j, :], op0=ALU.mult, op1=ALU.add)
                own(ins)
                v.tensor_tensor(h[:, 4:8, fr], h[:, 4:8, fr], zs[:, :, fr], ALU.mult).then_inc(gated, 1)
                n += 5
            dve.wait_ge(gated, NCH)
            for gr in range(2):
                norm([(h[:, 4 + 2 * gr + k, :],) * 2 for k in range(2)], lambda k: pr("gn", 2 * gr + k))

            def cross_and_ffn(l):
                norm_x(f"cross{l}")
                dve.wait_ge(outs, 16 * (ODD_OUTS if l else SCAN_OUTS))
                own(v.memset(xqb, 0.0))
                for j in range(4):
                    norm([(xq[:, j, :],) * 2], lambda _: pr(f"xq{l}"))
                dve.wait_ge(applied, APPLIED[f"q{l}.3"])
                for hh in range(MH):
                    ins = v.tensor_copy(xqb[:, :, hh * 80:hh * 80 + STEP], runs(xq[:, hh, SEQ:T]))
                ins.then_inc(qblk_ready, 1)
                first = (NX + NFOX) * l

                def maxima(it):
                    b, i = it % 2, first + it
                    dve.wait_ge(S_done, 2 * NCH + i + 1)
                    own(v.tensor_reduce(stats[:, b, 0:2], S[:, b, :].rearrange("p (s m) -> p s m", s=2),
                                        AX_X, ALU.max))
                    v.tensor_scalar(stats[:, b, 2:4], stats[:, b, 0:2], -SCALE_X, None, ALU.mult)\
                        .then_inc(neg_ready, 1)

                def normalise(it):
                    b, i = it % 2, first + it
                    dve.wait_ge(S_read[b], NCH + i // 2 + 1)
                    own(v.reciprocal(stats[:, b, 6:8], stats[:, b, 4:6]))
                    v.tensor_tensor(xP[:, b, :, :], xP[:, b, :, :],
                                    stats[:, b, 6:8].unsqueeze(2).broadcast_to([P, 2, MT]), ALU.mult)\
                        .then_inc(prob_ready, 1)

                def results(it):
                    n = TILE0[f"xo{l}"] + it
                    tile_wait(dve, n)
                    o = G[n % 2]
                    if it < 8:
                        qt, hh = it // 2, 2 * (it % 2)
                        ins = v.tensor_copy(xo[:, hh:hh + 2, qt * P:(qt + 1) * P],
                                            o[:, 0:2 * P].rearrange("p (s q) -> p s q", s=2))
                    else:
                        for sl in range(2):
                            at = SEQ + (2 * (it - 8) + sl) * 2 * STEP
                            for e in range(2):
                                src = o[:, sl * P + e * 64:sl * P + e * 64 + 64]
                                ins = v.tensor_copy(xo[:, :, at + e * STEP:at + (e + 1) * STEP],
                                                    src.rearrange("p (h t) -> p h t", h=MH))
                    ins.then_inc(read[n % 2], 1)

                for it in range(NX + 3):
                    if it < NX:
                        maxima(it)
                    if 1 <= it <= NX:
                        normalise(it - 1)
                    if it >= 3:
                        results(it - 3)
                add_residual(f"wo{l}", lambda j: j == 5 and [low_part(f"up{l}a", 0, s) for s in range(2)])
                m = nnorm[0]
                dve.wait_ge(rstd_ready, m + 1)
                for k in range(KD + 1):
                    if k < KD:
                        if k >= 4:
                            dve.wait_ge(applied, APPLIED[f"ffn{l}"] - KD + k - 3)
                        v.scalar_tensor_tensor(out=raw_tile(k), in0=x[:, k, :], scalar=pr(f"ffn{l}", k),
                                               in1=rstd[:, m % 2, :], op0=ALU.mult, op1=ALU.mult).then_inc(h_raw, 1)
                    if k:
                        dve.wait_ge(h_hi, KD * l + k)
                        v.tensor_tensor(hs[:, 1, k - 1, :], raw_tile(k - 1), hs[:, 0, k - 1, :].bitcast(F32),
                                        ALU.subtract).then_inc(applied, 1)
                nnorm[0] += 1
                gf = gs[:, :, :, :].rearrange("p a k t -> p a (k t)")

                def gated_tile(j, n, step=0):
                    at = bass.ds(step * (RING * T) + j * T, T)
                    raw, hi, lo = tmp[:, j % 2, :], gf[:, 0, at], gf[:, 1, at]
                    own = step * (2 * RING) + (nself[0] + 2 * j)
                    dve.wait_ge(read[n % 2], step * RING + n // 2 + 1)
                    dve.wait_ge(tile_done, step * (2 * RING) + n + 2)
                    v.tensor_tensor(raw, raw, GF[(n + 1) % 2], ALU.mult).then_inc(dve_self, 1)
                    dve.wait_ge(dve_self, own + 1)
                    v.tensor_copy(hi, raw).then_inc(dve_self, 1)
                    dve.wait_ge(dve_self, own + 2)
                    v.tensor_tensor(lo, raw, hi.bitcast(F32), ALU.subtract).then_inc(read[(n + 1) % 2], 1)

                for half in "ab":
                    up, down = f"up{l}{half}", f"down{l}{half}"
                    t0 = TILE0[up]

                    def tiles(u, i=0):
                        nxt = (up, u + 1) if u < HALF - 1 else (down, 0)
                        low_part(*nxt, 0, i)
                        gated_tile(u, t0 + 2 * u, i)
                        low_part(*nxt, 1, i)

                    with dve.Fori(0, HALF // RING) as i:
                        for u in range(RING):
                            tiles(u, i)
                    for u in range(HALF // RING * RING, HALF):
                        tiles(u)
                    nself[0] += 2 * HALF
                    for j in range(KD):
                        n = TILE0[down] + j
                        nxt = (down, j + 1) if j < KD - 1 else (f"up{l}b", 0)
                        split_next = j < KD - 1 or half == "a"
                        if split_next:
                            low_part(*nxt, 0)
                        tile_wait(dve, n)
                        v.tensor_tensor(x[:, j, :], x[:, j, :], GF[n % 2], ALU.add).then_inc(read[n % 2], 1)
                        if split_next:
                            low_part(*nxt, 1)

            add_residual("evout")
            cross_and_ffn(0)
            norm_x("mix1")
            for j in range(4):
                n = TILE0["cgu"] + 2 * j
                read_wait(dve, n)
                tile_wait(dve, n + 1)
                if j == 0:
                    v.memset(cgu[:, :, 0:SW - 1], 0.0)
                a, b = padded(cgu, j, SW - 1, SPROMPT, SREQ, SW - 1)
                v.tensor_tensor(a, tmp[:, j % 2, 0:SEQ], G[(n + 1) % 2][:, 0:SEQ], ALU.mult)
                v.tensor_tensor(b, runs(tmp[:, j % 2, SEQ:T]), runs(G[(n + 1) % 2][:, SEQ:T]), ALU.mult)\
                    .then_inc(read[(n + 1) % 2], 1)
            n = TILE0["f"]
            tile_wait(dve, n)
            v.tensor_scalar(tmp[0:NH, 0, :], G[n % 2][0:NH, 0:T], pr("fb", 0, NH), None, ALU.add)\
                .then_inc(read[n % 2], 1)
            read_wait(dve, n)
            v.scalar_tensor_tensor(out=tmp[0:NH, 1, :], in0=tmp[0:NH, 0, :], scalar=-1.0, in1=tmp[0:NH, 0, :],
                                   op0=ALU.mult, op1=ALU.max).then_inc(f_abs, 1)
            dve.wait_ge(sc_in, 16 * 4)
            read_wait(dve, TILE0["cgu"] + 5)
            read_wait(dve, TILE0["cgu"] + 7)
            done = 0
            for w in range(SW):
                for i in range(8):
                    j = i // 2
                    out = (cacc[:, j, 0:SEQ], runs(cacc[:, j, SEQ:T]))[i % 2]
                    src = padded(cgu, j, 0, SPROMPT, SREQ, w)[i % 2]
                    if w == 0:
                        ins = v.tensor_scalar(out, src, pr("sw", j * SW), None, ALU.mult)
                    else:
                        dve.wait_ge(gbc, done - 7)
                        ins = v.scalar_tensor_tensor(out=out, in0=src, scalar=pr("sw", j * SW + w), in1=out,
                                                     op0=ALU.mult, op1=ALU.add)
                    ins.then_inc(gbc, 1)
                    done += 1
            dve.wait_ge(f_log, 1)
            v.scalar_tensor_tensor(out=fl, in0=tmp[0:NH, 0, :], scalar=0.0, in1=tmp[0:NH, 1, :],
                                   op0=ALU.min, op1=ALU.subtract).then_inc(f_ready, 1)
            dve.wait_ge(f_ready, 1)
            dve.wait_ge(flog_in, 16)
            own(v.tensor_copy(flog[:, :, PAST:KALL], runs(fl[:, SEQ:T])))
            v.tensor_tensor_scan(out=fcp, data0=one.broadcast_to([NH, SEQ]), data1=fl[:, 0:SEQ], initial=0.0,
                                 op0=ALU.mult, op1=ALU.add)
            for rq in range(REQ):
                ins = v.tensor_tensor_scan(out=fcr[:, rq, :], data0=one.broadcast_to([NH, KALL]), data1=flog[:, rq, :],
                                           initial=0.0, op0=ALU.mult, op1=ALU.add)
            ins.then_inc(fcum_ready, 1)
            v.memset(qblk, 0.0)
            dve.wait_ge(gbc, done)
            for j in range(4):
                n = TILE0["gb"] + j
                tile_wait(dve, n)
                v.tensor_tensor(cacc[:, j, :], cacc[:, j, :], G[n % 2][:, 0:T], ALU.mult).then_inc(read[n % 2], 1)
            for j in range(8):
                norm([(fqk[:, j, :],) * 2], lambda _: small[:, 4:5] if j < 4 else pr("fk"))
            dve.wait_ge(applied, APPLIED["fqk.7"])
            dve.wait_ge(fcum_ready, 1)

            def fox_queries(rq):
                b = rq % 2
                if rq >= 2:
                    dve.wait_ge(S_done, 2 * NCH + NX + 4 * NH + rq - 1)
                for e in range(2):
                    half = slice(64 * e, 64 * e + 64)
                    v.tensor_copy(qblk[half, b, :].rearrange("p (j s) -> p j s", s=160)
                                  [:, :, STEP * e:STEP * (e + 1)],
                                  fqk[half, 0:4, SEQ + rq * STEP:SEQ + (rq + 1) * STEP])
                v.tensor_tensor(fqd[:, b, :, :], cst("d8", NH).unsqueeze(2).broadcast_to([NH, NH, STEP]),
                                fcr[:, rq, PAST:KALL].unsqueeze(1).broadcast_to([NH, NH, STEP]), ALU.mult)\
                    .then_inc(qblk_ready, 1)

            def fox_width(it):
                return (FOX_ITEMS[it][1] + 1) * P if it < 4 * NH else 384

            def fox_maxima(it):
                b, i = it % 2, NX + it
                dve.wait_ge(S_done, 2 * NCH + i + 1)
                own(v.tensor_reduce(stats[:, b, 0:1], S[:, b, 0:fox_width(it)], AX_X, ALU.max))
                v.tensor_scalar(stats[:, b, 2:3], stats[:, b, 0:1], -1.0, None, ALU.mult).then_inc(neg_ready, 1)

            def fox_normalise(it):
                b, i, w = it % 2, NX + it, fox_width(it)
                dve.wait_ge(S_read[b], NCH + i // 2 + 1)
                own(v.reciprocal(stats[:, b, 6:7], stats[:, b, 4:5]))
                v.tensor_scalar(fP[:, b, 0:w], fP[:, b, 0:w], stats[:, b, 6:7], None, ALU.mult)\
                    .then_inc(prob_ready, 1)

            def fox_results(it):
                n = TILE0["fo"] + it
                tile_wait(dve, n)
                if it < 4 * NH:
                    hh, qt = FOX_ITEMS[it]
                    half = slice(64 * (hh % 2), 64 * (hh % 2) + 64)
                    ins = v.tensor_copy(h[half, 4 + hh // 2, qt * P:(qt + 1) * P], G[n % 2][half, 0:P])
                else:
                    at = SEQ + (it - 4 * NH) * STEP
                    for e in range(2):
                        half = slice(64 * e, 64 * e + 64)
                        ins = v.tensor_copy(h[half, 4:8, at:at + STEP],
                                            G[n % 2][half, 0:P].rearrange("p (j c) -> p j c", j=4)
                                            [:, :, STEP * e:STEP * (e + 1)])
                ins.then_inc(read[n % 2], 1)

            for it in range(NFOX + 3):
                if 0 <= it + 1 - 4 * NH < REQ:
                    fox_queries(it + 1 - 4 * NH)
                if it < NFOX:
                    fox_maxima(it)
                if 1 <= it <= NFOX:
                    fox_normalise(it - 1)
                if it >= 3:
                    fox_results(it - 3)
            add_residual("odout")
            cross_and_ffn(1)


def _feature_major(a):
    return a.T.reshape(-1, P, a.shape[0]).transpose(1, 0, 2)


def _cols(a):
    return a.reshape(-1, P).T


def _weights(w, width=256):
    K, N = w.shape
    return w.reshape(K // P, P, N // width, width).transpose(2, 1, 0, 3).reshape(N // width, P, -1)


def _paired(a, b):
    K = a.shape[0]
    return np.stack([a.reshape(K, -1, P), b.reshape(K, -1, P)], axis=2).reshape(K, -1)


def _constants():
    c = np.zeros((P, CONST["_"]), np.float32)

    def put(name, a):
        o = CONST[name][0]
        c[0:a.shape[0], o:o + a.shape[1]] = a

    i, j = np.arange(P)[:, None], np.arange(P)[None, :]
    eight = np.arange(NH)
    put("ident", i == j)
    put("ones", np.ones((P, P)))
    put("half", i // HD == j // HD)
    put("cmask", np.where(j <= i, 0.0, NEG))
    put("lmask", np.where(i <= j, 0.0, NEG))
    put("smask", np.where((i <= j) & (i // STEP == j // STEP), 0.0, NEG))
    put("d8", eight[:, None] == eight)
    put("nd8", np.where(eight[:, None] == eight, -1.0, 0.0))
    put("req", i // STEP == np.arange(REQ))
    put("negwin", np.where(np.arange(240) // STEP == REQ - 1, 0.0, NEG)[None, :])
    put("r16", i[:STEP] == j % STEP)
    put("m16", np.where(j[:, :STEP] <= i[:STEP], 0.0, NEG))
    put("sel", eight[:, None] == np.repeat(eight, HD))
    put("nd16", np.where(eight[:, None] == np.repeat(eight, STEP), -1.0, 0.0))
    return c


def kernel(**inputs):
    import concourse.bacc as bacc
    from concourse.bass_utils import run_bass_kernel_spmd

    a = {k: np.asarray(v) for k, v in inputs.items()}
    f32 = np.float32

    par = np.zeros((P, PAR["_"]), f32)

    def put(name, m):
        o = PAR[name][0]
        par[0:m.shape[0], o:o + m.shape[1]] = m

    for l in range(LAYERS):
        put(f"mix{l}", _cols(a["norm_mix_g"][l]))
        put(f"cross{l}", _cols(a["norm_cross_g"][l]))
        put(f"mem{l}", _cols(a["norm_mem_g"][l]))
        put(f"ffn{l}", _cols(a["norm_ffn_g"][l]))
        put(f"xq{l}", a["xa_q_norm_g"][l][:, None])
        put(f"xk{l}", a["xa_k_norm_g"][l][:, None])
    taps = lambda w: w.reshape(w.shape[0], -1, P).transpose(2, 1, 0).reshape(P, -1)
    put("cw", taps(a["conf_dw_w"][0]))
    put("cb", _cols(a["conf_dw_b"][0]))
    put("lng", _cols(a["conf_ln_g"][0]))
    put("lnb", _cols(a["conf_ln_b"][0]))
    put("xw", taps(a["ssd_conv_w"][0]))
    put("xb", _cols(a["ssd_conv_b"][0]))
    put("gn", _cols(a["ssd_norm_g"][0]))
    put("sw", taps(a["sconv_w"][0]))
    put("fq", np.tile(a["fox_q_norm_g"][0], 2)[:, None])
    put("fk", np.tile(a["fox_k_norm_g"][0], 2)[:, None])
    put("dskip", _cols(np.repeat(a["ssd_d"][0], HD)))
    put("dtb", a["ssd_dt_bias"][0][:, None])
    put("alog", a["ssd_a_log"][0][:, None])
    put("fb", a["fox_f_bias"][0][:, None])
    ev, od = a["ev_w_in"][0], a["od_w_in"][0]
    put("wdt", _weights(ev[:, 2560:], NH)[0])
    put("wf", _weights(od[:, 3072:], NH)[0])

    arrays = {
        "par": par,
        "const": _constants(),
        "x": _feature_major(np.concatenate([a["x_prompt"][0], a["x_sample"].reshape(NS, D)])),
        "mem": _feature_major(a["mem_prompt"][0]),
        "conf_state": a["state_conf_conv"][0].reshape(REQ, CW - 1, 4, P).transpose(3, 2, 0, 1),
        "xbc_state": a["state_ssd_conv"][0].reshape(REQ, XW - 1, KD, P).transpose(3, 2, 0, 1),
        "sc_state": a["state_sconv"][0].reshape(REQ, SW - 1, 4, P).transpose(3, 2, 0, 1),
        "ssd_state": a["state_ssd"][0].transpose(3, 0, 1, 2).reshape(P, REQ, 512),
        "fox_k": a["cache_fox_k"][0].reshape(REQ, PAST, 4, P).transpose(0, 3, 2, 1),
        "fox_v": a["cache_fox_v"][0].reshape(REQ, 2, P, 512).transpose(0, 2, 1, 3),
        "fox_logf": a["cache_fox_logf"][0].transpose(2, 0, 1),
        "mem_k": a["cache_mem_k"].reshape(LAYERS, 4, 2, MT, MH, P).transpose(0, 1, 5, 2, 4, 3),
        "mem_v": a["cache_mem_v"].reshape(LAYERS, 4, 2, 2, P, 512).transpose(0, 1, 4, 2, 3, 5),
        "w_glu": _weights(_paired(ev[:, 512:1024], ev[:, 0:512])),
        "w_z": _weights(ev[:, 1024:1536]),
        "w_xbc": _weights(ev[:, 1536:2560]),
        "w_evout": _weights(a["ev_w_out"][0]),
        "w_cgu": _weights(_paired(od[:, 1024:1536], od[:, 0:512])),
        "w_gb": _weights(od[:, 512:1024]),
        "w_fqk": _weights(od[:, 1536:2560]),
        "w_fv": _weights(od[:, 2560:3072]),
        "w_odout": _weights(a["od_w_out"][0]),
    }
    for l in range(LAYERS):
        arrays[f"w_mk{l}"] = _weights(a["xa_wk"][l])
        arrays[f"w_mv{l}"] = _weights(a["xa_wv"][l])
        arrays[f"w_q{l}"] = _weights(a["xa_wq"][l])
        arrays[f"w_wo{l}"] = _weights(a["xa_wo"][l])
        w1 = _weights(_paired(a["ffn_w1"][l], a["ffn_w3"][l]))
        w2 = a["ffn_w2"][l].reshape(2, HALF, P, KD, P).transpose(0, 3, 2, 1, 4).reshape(2, KD, P, HALF * P)
        for i, half in enumerate("ab"):
            arrays[f"w_up{l}{half}"] = w1[i * HALF:(i + 1) * HALF]
            arrays[f"w_down{l}{half}"] = w2[i]
    out_shapes = {
        "o_y": (P, KD, T),
        "o_conf_p": (P, 4, CW - 1), "o_conf_s": (P, 4, REQ, CW - 1),
        "o_xbc_p": (P, KD, XW - 1), "o_xbc_s": (P, KD, REQ, XW - 1),
        "o_ssd_p": (P, 512), "o_ssd_s": (P, REQ, 512),
        "o_sc_p": (P, 4, SW - 1), "o_sc_s": (P, 4, REQ, SW - 1),
        "o_fk": (P, 4, T), "o_fv": (P, NCH, 512), "o_fl": (NH, T),
        "o_mk": (P, LAYERS, MH, MT), "o_mv": (P, LAYERS, 2, 512),
    }
    nc = bacc.Bacc("TRN2", target_bir_lowering=False, num_devices=1)
    arrays = {k: np.ascontiguousarray(v) for k, v in arrays.items()}
    arrays = {f"in_{k}": v for k, v in arrays.items()}
    dram = {k[3:]: nc.dram_tensor(k, v.shape, F32, kind="ExternalInput").ap() for k, v in arrays.items()}
    for k, s in out_shapes.items():
        dram[k] = nc.dram_tensor(k, s, F32, kind="ExternalOutput").ap()
    build(nc, dram)
    r = run_bass_kernel_spmd(nc, [arrays], core_ids=[0]).results[0]
    r = {k: np.asarray(r[k]) for k in out_shapes}

    y = r["o_y"].transpose(2, 1, 0).reshape(T, D)
    prompt_state = lambda s: s.transpose(2, 1, 0).reshape(1, 1, s.shape[2], -1)
    run_state = lambda s: s.transpose(2, 3, 1, 0).reshape(1, REQ, s.shape[3], -1)
    fk = r["o_fk"].transpose(2, 1, 0).reshape(T, NH, HD)
    fv = r["o_fv"].transpose(1, 0, 2).reshape(T, NH, HD)
    fl = r["o_fl"].T
    return tuple(np.ascontiguousarray(v) for v in (
        y[:SEQ].reshape(1, SEQ, D), y[SEQ:].reshape(REQ, STEP, D),
        prompt_state(r["o_conf_p"]), run_state(r["o_conf_s"]),
        prompt_state(r["o_xbc_p"]), run_state(r["o_xbc_s"]),
        r["o_ssd_p"].T.reshape(1, 1, NH, HD, P),
        r["o_ssd_s"].transpose(1, 2, 0).reshape(1, REQ, NH, HD, P),
        prompt_state(r["o_sc_p"]), run_state(r["o_sc_s"]),
        fk[:SEQ].reshape(1, 1, SEQ, NH, HD), fk[SEQ:].reshape(1, REQ, STEP, NH, HD),
        fv[:SEQ].reshape(1, 1, SEQ, NH, HD), fv[SEQ:].reshape(1, REQ, STEP, NH, HD),
        fl[:SEQ].reshape(1, 1, SEQ, NH), fl[SEQ:].reshape(1, REQ, STEP, NH),
        r["o_mk"].transpose(1, 3, 2, 0).reshape(LAYERS, 1, MT, MH, P),
        r["o_mv"].transpose(1, 2, 0, 3).reshape(LAYERS, 1, MT, MH, P),
    ))
```

```python
from contextlib import ExitStack

import numpy as np

import concourse.bass as bass
from concourse import mybir

F32 = mybir.dt.float32
F32R = mybir.dt.float32r
ALU = mybir.AluOpType
ACT = mybir.ActivationFunctionType
AX_X = mybir.AxisListType.X

P = 128
D = 1024
KD = D // P
SEQ, REQ, STEP = 512, 8, 16
NS = REQ * STEP
T = SEQ + NS
PAST = 256
HID = 2816
KH = HID // P
HALF = KH // 2
KS = 6
CONF, CW = 512, 31
XBC, XW = 1024, 4
SC, SW = 512, 3
NH = 8
HD = 64
MH, MT = 4, 256
CPROMPT, CREQ = CW - 1 + SEQ, CW - 1 + STEP
CONF_ROW = CPROMPT + REQ * CREQ
XPROMPT, XREQ = XW - 1 + SEQ, XW - 1 + STEP
XBC_ROW = XPROMPT + REQ * XREQ
SPROMPT, SREQ = SW - 1 + SEQ, SW - 1 + STEP
SC_ROW = SPROMPT + REQ * SREQ
NCH = T // P
NSEG = SEQ // P + REQ
KALL = PAST + STEP
NEG = -1e30
RING = 4
WCH = 2048
LAYERS = 2

CONST = {}


def _place(table, name, n):
    table[name] = (table.get("_", 0), n)
    table["_"] = table.get("_", 0) + n


for _n, _w in (("ident", P), ("ones", P), ("half", P), ("cmask", P), ("lmask", P), ("smask", P),
               ("d8", NH), ("sel", 4 * P), ("nd16", P), ("req", REQ), ("negwin", 240), ("r16", P), ("m16", STEP)):
    _place(CONST, _n, _w)
PAR = {}
for _n, _w in (("mix0", KD), ("mix1", KD), ("cross0", KD), ("cross1", KD), ("mem0", KD), ("mem1", KD),
               ("ffn0", KD), ("ffn1", KD), ("cw", 4 * CW), ("cb", 4), ("lng", 4), ("lnb", 4),
               ("xw", KD * XW), ("xb", KD), ("gn", 4), ("sw", 4 * SW), ("fq", 1), ("fk", 1),
               ("xq0", 1), ("xq1", 1), ("xk0", 1), ("xk1", 1), ("dskip", 4),
               ("dtb", 1), ("alog", 1), ("fb", 1), ("wdt", KD * NH), ("wf", KD * NH)):
    _place(PAR, _n, _w)

SCAN_TILES = 5 * (NCH - 1) + 4 + REQ
TILE = {}
for _n, _c in (("glu", 8), ("mk0", 4), ("mv0", 2), ("mk1", 4), ("mv1", 2), ("xbc", 8), ("dt", 1), ("z", 4),
               ("tok", 2), ("scan", SCAN_TILES), ("evout", 8),
               ("q0", 4), ("xo0", 10), ("wo0", 8), ("up0a", KH), ("down0a", 8), ("up0b", KH), ("down0b", 8),
               ("f", 1), ("fv", NCH), ("cgu", 8), ("gb", 4), ("fqk", 8),
               ("fo", 4 * NH + REQ), ("odout", 8),
               ("q1", 4), ("xo1", 10), ("wo1", 8), ("up1a", KH), ("down1a", 8), ("up1b", KH), ("down1b", 8)):
    _place(TILE, _n, _c)
TILE0 = {k: v[0] for k, v in TILE.items() if k != "_"}

APPLIED, NORM, _a, _m = {}, [], 0, 0
for _n, _c in ([("mix0", 8), ("mem", 16)] + [(f"mk{l}.{j}", 0) for l in range(2) for j in range(4)]
               + [("mean", 4), ("var", 4), ("gn0", 2), ("gn1", 2), ("cross0", 8)]
               + [(f"q0.{j}", 1) for j in range(4)] + [("ffn0", 8), ("mix1", 8)]
               + [(f"fqk.{j}", 1) for j in range(8)] + [("cross1", 8)]
               + [(f"q1.{j}", 1) for j in range(4)] + [("ffn1", 8)]):
    _a, _m = _a + _c, _m + (_c == 0)
    APPLIED[_n] = _a
    NORM.append((_c == 0, _m if _c == 0 else _a))


SUMMED, _s = [], 0
for _squares, _sums in ([(8, 8)] * 2 + [(1, 1)] * 8 + [(0, 4), (4, 4), (2, 2), (2, 2), (8, 2)] + [(1, 1)] * 4
                        + [(8, 2)] * 2 + [(1, 1)] * 8 + [(8, 2)] + [(1, 1)] * 4 + [(8, 2)]):
    SUMMED += [_s + max(1, k + 1 - _squares + _sums) for k in range(_squares)]
    _s += _sums
SUM_ADDS = KD - 2
SQUARE0 = {"evout": 32, "wo0": 44, "down0b": 52, "odout": 68, "wo1": 80}


CHUNKS, CHUNK, PIECE0 = [], {}, {"_": 0}


def _chunks(name, count, width, ends):
    CHUNK[name] = len(CHUNKS)
    CHUNKS.extend(("w_" + name, i, width, ends(i)) for i in range(count))


def _pairs(tile):
    return lambda i: TILE0[tile] + 2 * i + 2


def _cross_ffn(l):
    _chunks("q" + l, 2, WCH, _pairs("q" + l))
    _chunks("wo" + l, 4, 4 * 256, _pairs("wo" + l))
    for half in "ab":
        for name in ("up" + l + half, "down" + l + half):
            PIECE0[name] = PIECE0["_"]
            count, width = (HALF, WCH) if name[0] == "u" else (KD, HALF * P)
            PIECE0["_"] += 2 * count
            _chunks(name, count, width, lambda i: -(PIECE0[name] + 2 * i + 2))


_chunks("glu", 4, WCH, _pairs("glu"))
for _l in "01":
    _chunks("mk" + _l, 2, WCH, _pairs("mk" + _l))
    _chunks("mv" + _l, 2, WCH, lambda i, t="mv" + _l: TILE0[t] + 2)
_chunks("xbc", 4, WCH, _pairs("xbc"))
_chunks("z", 2, WCH, _pairs("z"))
_chunks("evout", 4, WCH, _pairs("evout"))
_cross_ffn("0")
_chunks("fv", 2, WCH, lambda i: TILE0["fv"] + NCH)
for _n, _c in (("cgu", 4), ("gb", 2), ("fqk", 4)):
    PIECE0[_n] = PIECE0["_"]
    PIECE0["_"] += 2 * _c
    _chunks(_n, _c, WCH, lambda i, p=PIECE0[_n]: -(p + 2 * i + 2))
_chunks("odout", 4, WCH, _pairs("odout"))
_cross_ffn("1")

FOX_ITEMS = [(h, qt) for h in range(NH) for qt in range(4)]
NFOX = 4 * NH + REQ
NX = 10
SCALE_X = 128 ** -0.5


def build(nc, dram):
    ctx = ExitStack()
    with ctx:
        def sb(name, shape):
            return ctx.enter_context(nc.sbuf_tensor(name, shape, F32))

        def sem(name):
            return ctx.enter_context(nc.semaphore(name))

        const = sb("const", [P, CONST["_"]])
        par = sb("par", [P, PAR["_"]])

        def cst(name, rows=P):
            o, n = CONST[name]
            return const[0:rows, o:o + n]

        def pr(name, i=0, rows=P):
            o = PAR[name][0] + i
            return par[0:rows, o:o + 1]

        x = sb("resid", [P, KD, T])
        ring = sb("ring", [P, RING, WCH])
        work = sb("work", [P, 4, T])
        sq = work[:, 0:2, :]
        rstd = sb("rstd", [P, 2, T])
        tmp = work[:, 2:4, :]
        mkT = sb("mkT", [P, LAYERS, MH, MT])
        mv = sb("mv", [P, LAYERS, 2, 512])
        small = sb("small", [P, 8])
        stats = sb("stats", [P, 2, 8])
        csend = sb("csend", [NH, NSEG])
        cdiag = sb("cdiag", [NH, NSEG, NH])
        decay = sb("decay", [P, NSEG, NH])
        toks = sb("toks", [P, 2, NCH, NH])
        ARENA = 24064
        with nc.sbuf_tensor("front", [P, KD * T + ARENA], F32) as front:
            h = front[:, 0:KD * T].rearrange("p (k t) -> p k t", k=KD)
            arena = front[:, KD * T:]
        CGU_AT, HS1_AT = KD * T // 2, KD * T // 2 + 4 * SC_ROW
        with ExitStack() as over:
            over.enter_context(nc.sbuf_tensor("gated_rows", [P, HS1_AT], F32))
            hs1 = over.enter_context(nc.sbuf_tensor("h1_split", [P, 2, KD, T], F32R))
            ws1 = over.enter_context(nc.sbuf_tensor("w1_split", [P, 2, 2, KD * P], F32R))
        hs = ctx.enter_context(nc.sbuf_tensor("h_split", [P, 2, KD, T], F32R))
        gs = ctx.enter_context(nc.sbuf_tensor("g_split", [P, 2, HALF, T], F32R))
        ws = ctx.enter_context(nc.sbuf_tensor("w_split", [P, 2, 2, KD * P], F32R))
        assert 2 * KD * T + 2 * HALF * T + 4 * KD * P <= KD * T + ARENA

        class Region:

            def __init__(self, at=0):
                self.at = at

            def __call__(self, *shape, rows=P):
                n = int(np.prod(shape))
                v = arena[0:rows, self.at:self.at + n]
                self.at += n
                assert self.at <= ARENA, self.at
                names = "abcd"[:len(shape)]
                if len(shape) > 1:
                    v = v.rearrange(f"p ({' '.join(names)}) -> p {' '.join(names)}",
                                    **{c: s for c, s in zip(names[1:], shape[1:])})
                return v

        r = Region()
        aglu = r(4, CONF_ROW)
        xbcp = r(KD, XBC_ROW)
        scan_room = r.at
        zs = r(4, T)
        memx = arena[:, scan_room:scan_room + KD * MT].rearrange("p (k m) -> p k m", k=KD)
        acc = r(4, T)
        xbcc = r(KD, T)
        xbcc_at = r.at - KD * T
        memh = arena[:, xbcc_at:xbcc_at + LAYERS * KD * MT].rearrange("p (l k m) -> p l k m", l=LAYERS, k=KD)
        hT = r(512)
        xdt = r(512)
        xdte = r(512)
        btok = r(256)
        dtb = r(4, T, rows=NH)
        r = Region()
        h0T = r(REQ, 512)
        bmask = r(REQ, 256)
        Lm = r(NH, P)
        ysc = r(4, P)
        assert r.at <= scan_room
        r = Region(scan_room + 4 * T)
        Pm = r(NH, P)
        Ee = r(4, P)
        assert r.at <= xbcc_at
        r = Region()
        cacc = h[:, 0:4, :]
        cgu = front[:, CGU_AT:HS1_AT].rearrange("p (j s) -> p j s", j=4)
        r = Region(HS1_AT - KD * T + 2 * KD * T + 4 * KD * P)
        fqk = r(8, T)
        fv = r(NCH, 512)
        fcp = r(SEQ, rows=NH)
        fl = r(T, rows=NH)
        fx = r(T, rows=NH)
        split_end = HS1_AT + KD * T + 4 * KD * P
        r = Region(HS1_AT - KD * T)
        kc = r(2, 4, PAST)
        vc = r(2, 2, 512)
        qblk = r(2, 640)
        flog = r(REQ, KALL, rows=NH)
        fcr = r(REQ, KALL, rows=NH)
        fqd = r(2, NH, STEP, rows=NH)
        BR = 32 + NH
        fdif = r(2, 2, SEQ)
        assert r.at <= split_end
        r = Region()
        xq = r(4, T)
        xo = r(4, T)
        xkc = r(4, 2, MH, MT)
        xvc = r(4, 2, 2, 512)
        xqb = r(REQ, 320)
        wf = work[:, :, :].rearrange("p a b -> p (a b)")
        fP = wf[:, 0:3 * 512].rearrange("p (b m) -> p b m", b=3)
        xP = wf[:, 0:3 * 512].rearrange("p (b s m) -> p b s m", b=3, s=2)
        fPT = xPT = wf[:, 3 * 512:5 * 512].rearrange("p (b k m) -> p b k m", b=2, k=4)
        assert 5 * 512 <= 4 * T

        G = [ctx.enter_context(nc.psum_tensor(f"G{i}", [P, 1024], F32)) for i in range(2)]
        S = ctx.enter_context(nc.psum_tensor("S", [P, 2, 512], F32))
        Q = ctx.enter_context(nc.psum_tensor("Q", [P, 2, 512], F32))
        QF = Q[:, :, :].rearrange("p a b -> p (a b)")
        HT = T // 2
        GF = [G[i][:, 512 - HT:512 + HT] for i in range(2)]

        high, split = sem("high"), sem("split")
        half_used = sem("half_used")
        h1_hi, h1_split = sem("h1_hi"), sem("h1_split")
        h_raw, h_hi = sem("h_raw"), sem("h_hi")
        const_in, par_in, mem_in, pads_in = map(sem, ("const_in", "par_in", "mem_in", "pads_in"))
        x_in = [sem(f"x_in{i}") for i in range(KD // 2)]
        chunk_in = [sem(f"chunk_in{i}") for i in range(RING)]
        tile_done = sem("tile_done")
        read = [sem(f"read{i}") for i in range(2)]
        S_done, Q_done = sem("S_done"), sem("Q_done")
        S_read = [sem(f"S_read{i}") for i in range(2)]
        Q_read = [sem(f"Q_read{i}") for i in range(2)]
        act_self, dve_self = sem("act_self"), sem("dve_self")
        sq_ready, sq_used = sem("sq_ready"), sem("sq_used")
        added = sem("added")
        stat_read, rstd_ready = sem("stat_read"), sem("rstd_ready")
        applied = sem("applied")
        mk_applied, pool_self = sem("mk_applied"), sem("pool_self")
        small_ready, outs = sem("small_ready"), sem("outs")
        conv, xconv, xbc_done = sem("conv"), sem("xconv"), sem("xbc_done")
        mixed = sem("mixed")
        dt_abs, dt_log, cs_ready, de_ready = map(sem, ("dt_abs", "dt_log", "cs_ready", "de_ready"))
        state_in, xdte_ready, gated, hT_zero = map(sem, ("state_in", "xdte_ready", "gated", "hT_zero"))
        fdif_ready = sem("fdif_ready")
        neg_ready, prob_ready, qblk_ready = map(sem, ("neg_ready", "prob_ready", "qblk_ready"))
        keys_in = [sem(f"keys_in{i}") for i in range(2)]
        values_in = [sem(f"values_in{i}") for i in range(2)]
        xcache_in = [sem(f"xcache_in{i}") for i in range(4)]
        sc_in, flog_in, f_abs, f_log, f_ready, fcum_ready, gbc = map(
            sem, ("sc_in", "flog_in", "f_abs", "f_log", "f_ready", "fcum_ready", "gbc"))

        block = ctx.enter_context(nc.Block())

        CONV_OUTS = 8 + 16
        SCAN_OUTS = CONV_OUTS + 2 + 2
        ODD_OUTS = SCAN_OUTS + 8 + 3

        def tile_wait(eng, n):
            eng.wait_ge(tile_done, n + 1)

        def read_wait(eng, n):
            eng.wait_ge(read[n % 2], n // 2 + 1)

        def padded(buf, j, pad, prompt, req, off):
            a = buf[:, j, off:off + SEQ]
            b = buf[:, j, prompt:prompt + REQ * req].rearrange("p (r t) -> p r t", r=REQ)
            return a, b[:, :, off:off + STEP]

        def raw_tile(k):
            return (tmp, sq)[k // 2 % 2][:, k % 2, :]

        def piece(name, u, s):
            up, buf = name[0] != "d", ws if name[0] in "ud" else ws1
            w = ring[:, (CHUNK[name] + u) % RING, 0:WCH if up else HALF * P]\
                .rearrange("p (k n) -> p k n", k=KD if up else HALF)
            src = w[:, :, s * P:(s + 1) * P] if up else w[:, s * KS:HALF if s else KS]
            KT = src.shape[1]
            parts = [buf[:, s, part, 0:KT * P].rearrange("p (k n) -> p k n", k=KT) for part in range(2)]
            return src, parts[0], parts[1]

        PIECES1 = [(name, j // 2, j % 2) for name, n in (("cgu", 8), ("gb", 4), ("fqk", 8)) for j in range(n)]

        def runs(ap):
            return ap.rearrange("p (r t) -> p r t", r=REQ)

        @block.sync
        def _(sp):
            sp.dma_start(const[:, :], dram["const"]).then_inc(const_in, 16)
            for k in range(0, KD, 2):
                sp.dma_start(x[:, k:k + 2, :], dram["x"][:, k:k + 2, :]).then_inc(x_in[k // 2], 16)
            sp.dma_start(par[:, :], dram["par"]).then_inc(par_in, 16)

            def load(c, idx, free):
                array, _, width, _ = CHUNKS[c]
                if free is not None:
                    done, count = free
                    sp.wait_ge(done, count)
                sp.dma_start(ring[:, c % RING, 0:width], dram[array][idx].rearrange("a p n -> (a p) n"))\
                    .then_inc(chunk_in[c % RING], 16)

            def slot_free(c):
                if c < RING:
                    return None
                count = CHUNKS[c - RING][3]
                return (tile_done, count) if count > 0 else (split, -count)

            c = 0
            while c < len(CHUNKS):
                name, idx = CHUNKS[c][0][2:], CHUNKS[c][1]
                if name.startswith(("up", "down")):
                    count = HALF if name[0] == "u" else KD
                    for u in range(RING):
                        load(c + u, slice(u, u + 1), slot_free(c + u))
                    loops = count // RING
                    with sp.Fori(1, loops) as i:
                        for u in range(RING):
                            load(c + u, bass.ds(i * RING + u, 1),
                                 (split, i * (2 * RING) + (PIECE0[name] + 2 * (u + 1 - RING))))
                    for u in range(loops * RING, count):
                        load(c + u, slice(u, u + 1), slot_free(c + u))
                    c += count
                else:
                    load(c, slice(idx, idx + 1), slot_free(c))
                    c += 1

        @block.gpsimd
        def _(pool):
            stores = [0]

            def store(dst, src):
                pool.dma_start(dst, src).then_inc(outs, 16)
                stores[0] += 1

            def stores_landed():
                pool.wait_ge(outs, 16 * stores[0])

            pool.wait_ge(x_in[-1], 16)
            pool.dma_start(memx, dram["mem"]).then_inc(mem_in, 16)
            for j in range(4):
                pool.dma_start(aglu[:, j, CPROMPT:].rearrange("p (r t) -> p r t", r=REQ)[:, :, 0:CW - 1],
                               dram["conf_state"][:, j]).then_inc(pads_in, 16)
            for j in range(KD):
                pool.dma_start(xbcp[:, j, XPROMPT:].rearrange("p (r t) -> p r t", r=REQ)[:, :, 0:XW - 1],
                               dram["xbc_state"][:, j]).then_inc(pads_in, 16)
            pool.wait_ge(pads_in, 16 * 12)
            for j in range(4):
                read_wait(pool, TILE0["glu"] + 2 * j + 1)
                store(dram["o_conf_p"][:, j], aglu[:, j, SEQ:SEQ + CW - 1])
                store(dram["o_conf_s"][:, j], aglu[:, j, CPROMPT:].rearrange(
                    "p (r t) -> p r t", r=REQ)[:, :, STEP:])
            for i in range(LAYERS * MH):
                key = mkT[:, i // MH, i % MH, :]
                pool.wait_ge(rstd_ready, i + 3)
                nc.gpsimd.tensor_tensor(key, key, rstd[:, i % 2, 0:MT], ALU.mult).then_inc(pool_self, 1)
                pool.wait_ge(pool_self, i + 1)
                nc.gpsimd.tensor_scalar(key, key, pr(f"xk{i // MH}"), 1.0, ALU.mult, ALU.mult)\
                    .then_inc(mk_applied, 1)
            for j in range(KD):
                read_wait(pool, TILE0["xbc"] + j)
                store(dram["o_xbc_p"][:, j], xbcp[:, j, SEQ:SEQ + XW - 1])
                store(dram["o_xbc_s"][:, j], xbcp[:, j, XPROMPT:].rearrange(
                    "p (r t) -> p r t", r=REQ)[:, :, STEP:])
            stores_landed()
            pool.wait_ge(xbc_done, KD)
            pool.dma_start(h0T, dram["ssd_state"]).then_inc(state_in, 16)
            pool.wait_ge(mk_applied, LAYERS * MH)
            store(dram["o_mk"], mkT[:, :, :, :])
            read_wait(pool, TILE0["mv1"])
            read_wait(pool, TILE0["mv1"] + 1)
            store(dram["o_mv"], mv[:, :, :, :])
            last = TILE0["scan"] + SCAN_TILES - 1
            read_wait(pool, TILE0["scan"] + 5 * (NCH - 1) - 1)
            store(dram["o_ssd_p"], hT)
            read_wait(pool, last)
            read_wait(pool, last - 1)
            store(dram["o_ssd_s"], h0T)
            stores_landed()
            assert stores[0] == SCAN_OUTS

            def cross_caches(l, after):
                tile_wait(pool, after)
                for n in range(4):
                    pool.dma_start(xkc[:, n], dram["mem_k"][l, n]).then_inc(xcache_in[n], 16)
                    pool.dma_start(xvc[:, n], dram["mem_v"][l, n]).then_inc(xcache_in[n], 16)

            cross_caches(0, TILE0["evout"])
            for k in range(KD):
                pool.wait_ge(h1_hi, k + 1)
                nc.gpsimd.tensor_tensor(hs1[:, 1, k, :], h[:, k, :], hs1[:, 0, k, :].bitcast(F32), ALU.subtract)\
                    .then_inc(h1_split, 1)

            def low_part(q):
                pool.wait_ge(high, PIECE0["cgu"] + q + 1)
                name, u, s = PIECES1[q]
                src, hi, lo = piece(name, u, s)
                nc.gpsimd.tensor_tensor(lo, src, hi.bitcast(F32), ALU.subtract).then_inc(split, 1)

            low_part(0)
            low_part(1)
            pool.wait_ge(h1_split, KD)
            tile_wait(pool, TILE0["fv"] + NCH - 1)
            for j in range(4):
                pool.dma_start(cgu[:, j, SPROMPT:].rearrange("p (r t) -> p r t", r=REQ)[:, :, 0:SW - 1],
                               dram["sc_state"][:, j]).then_inc(sc_in, 16)
            for q in range(2, len(PIECES1)):
                low_part(q)
            tile_wait(pool, TILE0["fqk"] + 7)
            pool.dma_start(flog[:, :, 0:PAST], dram["fox_logf"]).then_inc(flog_in, 16)

            def fox_keys(rq):
                if rq >= 2:
                    pool.wait_ge(S_done, 2 * NCH + NX + 4 * NH + rq - 1)
                pool.dma_start(kc[:, rq % 2], dram["fox_k"][rq]).then_inc(keys_in[rq % 2], 16)

            def fox_values(rq):
                if rq >= 2:
                    tile_wait(pool, TILE0["fo"] + 4 * NH + rq - 2)
                pool.dma_start(vc[:, rq % 2], dram["fox_v"][rq]).then_inc(values_in[rq % 2], 16)

            for rq in range(2):
                fox_keys(rq)
                fox_values(rq)
            pool.wait_ge(sc_in, 16 * 4)
            for j in range(4):
                read_wait(pool, TILE0["cgu"] + 2 * j + 1)
                store(dram["o_sc_p"][:, j], cgu[:, j, SEQ:SEQ + SW - 1])
                store(dram["o_sc_s"][:, j], cgu[:, j, SPROMPT:].rearrange(
                    "p (r t) -> p r t", r=REQ)[:, :, STEP:])
            stores_landed()
            pool.wait_ge(applied, APPLIED["fqk.7"])
            store(dram["o_fk"], fqk[:, 4:8, :])
            for c in range(NCH):
                read_wait(pool, TILE0["fv"] + c)
            store(dram["o_fv"], fv)
            pool.wait_ge(f_ready, 1)
            store(dram["o_fl"], fl)
            fox_keys(2)
            fox_keys(3)
            for rq in range(2, REQ):
                if rq + 2 < REQ:
                    fox_keys(rq + 2)
                fox_values(rq)
            stores_landed()
            assert stores[0] == ODD_OUTS
            cross_caches(1, TILE0["odout"] + 7)
            for j in range(KD):
                read_wait(pool, TILE0["down1b"] + j)
                store(dram["o_y"][:, j], x[:, j, :])
            stores_landed()

        @block.tensor
        def _(pe):
            nsq, nready, nstat = [0], [0], [0]
            nS, nQ = [0, 0], [0, 0]

            def mm(out, lhsT, rhs, start, stop, **kw):
                return nc.tensor.matmul(out, lhsT, rhs, start=start, stop=stop, **kw)

            def chunk(c):
                pe.wait_ge(chunk_in[c % RING], 16 * (c // RING + 1))
                return c % RING

            def begin(n, before=None):
                pe.wait_ge(read[n % 2], n // 2 if before is None else before)
                return G[n % 2]

            def project(n, wslot, col, KT, rhs, cols=256, width=T, normed=None):
                out = begin(n)
                wide = min(512, width)
                for k in range(KT):
                    if normed is not None:
                        pe.wait_ge(applied, normed + k)
                    w = ring[:, wslot, k * cols + col:k * cols + col + P]
                    first, last = k == 0, k == KT - 1
                    m = mm(out[:, 0:wide], w, rhs(k)[:, 0:wide], first, last)
                    if width > 512:
                        m = mm(out[:, 512:width], w, rhs(k)[:, 512:width], first, last)
                m.then_inc(tile_done, 1)

            def split_product(n, slot, p, KT, rhs, weights=ws, before=None, normed=None, start=0, stop=True):
                if start == 0:
                    begin(n, before)
                out = GF[n % 2]
                pe.wait_ge(split, p + 1)
                for k in range(KT):
                    if normed is not None:
                        pe.wait_ge(applied, normed + k)
                    for wpart, xpart in ((0, 0), (0, 1), (1, 0)):
                        w = weights[:, slot, wpart, k * P:(k + 1) * P]
                        for f in range(2):
                            fr = slice(f * HT, (f + 1) * HT)
                            m = mm(out[:, fr], w, rhs[:, xpart, start + k, fr],
                                   k == 0 and start == 0 and wpart + xpart == 0,
                                   stop and k == KT - 1 and wpart == 1)
                m.then_inc(tile_done if stop else half_used, 1)

            def rows(buf):
                return lambda k: buf[:, k, :]

            def stat(k, tiles, ones, width=T, src=None):
                if k == 0:
                    pe.wait_ge(stat_read, nstat[0])
                    for b in range(2):
                        pe.wait_ge(Q_read[b], nQ[b])
                    nstat[0] += 1
                if src is None:
                    pe.wait_ge(sq_ready, nready[0] + 1)
                    src = sq[:, nready[0] % 2, :]
                    nready[0] += 1
                wide = min(512, width)
                m = mm(QF[:, 0:wide], ones, src[:, 0:wide], k == 0, k == tiles - 1)
                if width > 512:
                    m = mm(QF[:, 512:width], ones, src[:, 512:width], k == 0, k == tiles - 1)
                m.then_inc(sq_used, 1)

            def fill_S(b):
                pe.wait_ge(S_read[b], nS[b])
                nS[b] += 1

            def fill_Q(b):
                pe.wait_ge(Q_read[b], nQ[b])
                nQ[b] += 1

            pe.wait_ge(const_in, 16)
            ones, ident = cst("ones"), cst("ident")

            def projections(name, tiles, KT, rhs, cols=256, after=None, norm=None):
                normed = APPLIED[norm] - KD + 1 if norm else None
                for n in range(tiles):
                    if n % 2 == 0:
                        s = chunk(CHUNK[name] + n // 2)
                    project(TILE0[name] + n, s, n % 2 * P, KT, rhs, cols=cols, normed=None if n else normed)
                    if after:
                        after(n)

            def residual_stat(norms):
                pe.wait_ge(added, SUM_ADDS * (norms + 1))
                nready[0] += KD - 1
                stat(0, 2, ones, src=rstd[:, nstat[0] % 2, :])
                stat(1, 2, ones)

            def narrow(name, wname, normed=None):
                out = begin(TILE0[name])
                pe.wait_ge(par_in, 16)
                o = PAR[wname][0]
                for k in range(KD):
                    if normed is not None:
                        pe.wait_ge(applied, normed + k)
                    w = par[:, o + k * NH:o + (k + 1) * NH]
                    mm(out[0:NH, 0:512], w, h[:, k, 0:512], k == 0, k == KD - 1)
                    m = mm(out[0:NH, 512:T], w, h[:, k, 512:T], k == 0, k == KD - 1)
                m.then_inc(tile_done, 1)

            def frame_major(n, lhs, sa, sc):
                out = begin(n)
                for k in range(KD):
                    mm(out[:, 0:256], lhs(k), ring[:, sa, k * 256:(k + 1) * 256], k == 0, k == KD - 1,
                       skip_group_check=True)
                    m = mm(out[:, 256:512], lhs(k), ring[:, sc, k * 256:(k + 1) * 256], False, k == KD - 1,
                           skip_group_check=True)
                m.then_inc(tile_done, 1)

            for k in range(KD):
                stat(k, KD, ones)
            projections("glu", 8, KD, rows(h), norm="mix0",
                        after=lambda n: n == 1 and [stat(k, KD, ones, MT) for k in range(KD)])
            for l in range(LAYERS):
                for n in range(4):
                    if n % 2 == 0:
                        s = chunk(CHUNK[f"mk{l}"] + n // 2)
                    project(TILE0[f"mk{l}"] + n, s, n % 2 * P, KD, lambda k, l=l: memh[:, l, k, :], width=MT)
                    if n:
                        stat(0, 1, ones, MT)
                stat(0, 1, ones, MT)
                sa, sc = chunk(CHUNK[f"mv{l}"]), chunk(CHUNK[f"mv{l}"] + 1)
                for m2 in range(2):
                    frame_major(TILE0[f"mv{l}"] + m2, lambda k: memh[:, l, k, m2 * P:(m2 + 1) * P], sa, sc)
            projections("xbc", 8, KD, rows(h))
            narrow("dt", "wdt")
            projections("z", 4, KD, rows(h))
            pe.wait_ge(conv, 8 * CW)
            for k in range(4):
                stat(k, 4, ones, src=acc[:, k, :])
            n = TILE0["tok"]
            out = begin(n)
            pe.wait_ge(de_ready, 1)
            for v in range(2):
                for c in range(NCH):
                    at = (v * NCH + c) * NH
                    m = nc.tensor.transpose(out[:, at:at + NH], dtb[:, 1 + v, c * P:(c + 1) * P],
                                            ident[0:NH, 0:NH])
            m.then_inc(tile_done, 1)
            out = begin(n + 1)
            mm(out[:, 0:NSEG * NH], ones[0:NH, :], cdiag[:, :, :].rearrange("p a b -> p (a b)"), True, True)\
                .then_inc(tile_done, 1)
            for k in range(4):
                stat(k, 4, ones)
            n = TILE0["scan"]
            d8, sel = cst("d8", NH), cst("sel", NH)
            pe.wait_ge(xbc_done, KD)
            for c in range(NCH):
                fr = slice(c * P, (c + 1) * P)
                run = c == NCH - 1
                out = begin(n)
                for j in range(4):
                    m = nc.tensor.transpose(out[:, j * P:(j + 1) * P], xbcc[:, j, fr], ident)
                m.then_inc(tile_done, 1)
                out = begin(n + 1)
                for j in range(2):
                    m = nc.tensor.transpose(out[:, j * P:(j + 1) * P], xbcc[:, 4 + j, fr], ident)
                m.then_inc(tile_done, 1)
                if c == 0:
                    pe.wait_ge(stat_read, nstat[0])
                fill_Q(0)
                for gr in range(2):
                    m = mm(Q[:, 0, gr * P:(gr + 1) * P], xbcc[:, 4 + gr, fr], xbcc[:, 6 + gr, fr], True, True)
                m.then_inc(Q_done, 1)
                mask = cst("smask" if run else "lmask")
                for gr in range(2):
                    fill_S(gr)
                    o = S[:, gr, :].rearrange("p (h l) -> p h l", h=4)
                    mm(o, ident, mask.unsqueeze(1).broadcast_to([P, 4, P]), True, False, skip_group_check=True)
                    mm(o, dtb[:, 0, fr], d8[:, 4 * gr:4 * gr + 4].unsqueeze(2).broadcast_to([NH, 4, P]),
                       False, False, skip_group_check=True)
                    for hh in range(4):
                        m = mm(o[:, hh, :], d8[:, 4 * gr + hh:4 * gr + hh + 1].broadcast_to([NH, P]),
                               dtb[:, 3, fr], False, hh == 3, skip_group_check=True)
                    m.then_inc(S_done, 1)
                fill_Q(1)
                for j in range(4):
                    m = mm(Q[:, 1, j * P:(j + 1) * P],
                           sel[:, j * P:(j + 1) * P], dtb[:, 3, fr], True, True)
                m.then_inc(Q_done, 1)
                out = begin(n + 2)
                read_wait(pe, n)
                pe.wait_ge(Q_read[0], nQ[0])
                for hh in range(NH):
                    e = hh % 2
                    m = mm(out[64 * e:64 * e + 64, hh // 2 * P:(hh // 2 + 1) * P],
                           xdt[:, hh * HD:(hh + 1) * HD], Pm[:, hh, :], True, True, skip_group_check=True)
                m.then_inc(tile_done, 1)
                out = begin(n + 3)
                if run:
                    pe.wait_ge(state_in, 16)
                    for rq in range(REQ):
                        for j in range(4):
                            at = SEQ + rq * STEP
                            m = mm(out[:, j * P + rq * STEP:j * P + (rq + 1) * STEP],
                                   h0T[:, rq, j * P:(j + 1) * P], xbcc[:, 6 + j // 2, at:at + STEP], True, True)
                else:
                    if c == 0:
                        pe.wait_ge(hT_zero, 1)
                    else:
                        read_wait(pe, n - 1)
                    for j in range(4):
                        m = mm(out[:, j * P:(j + 1) * P], hT[:, j * P:(j + 1) * P], xbcc[:, 6 + j // 2, fr],
                               True, True)
                m.then_inc(tile_done, 1)
                pe.wait_ge(xdte_ready, c + 1)
                read_wait(pe, n + 1)
                for k in range(REQ if run else 1):
                    out = begin(n + 4 + k)
                    for gr in range(2):
                        b = bmask[:, k, gr * P:(gr + 1) * P] if run else btok[:, gr * P:(gr + 1) * P]
                        m = mm(out[:, gr * 256:(gr + 1) * 256], b, xdte[:, gr * 256:(gr + 1) * 256], True, True)
                    m.then_inc(tile_done, 1)
                n += 5
            for gr in range(2):
                for k in range(2):
                    stat(k, 2, ones)

            def cross_and_ffn(l):
                residual_stat(3 * l)
                projections(f"q{l}", 4, KD, rows(h), norm=f"cross{l}", after=lambda n: n and stat(0, 1, ones))
                stat(0, 1, ones)
                pe.wait_ge(applied, APPLIED[f"q{l}.3"])
                pe.wait_ge(stat_read, nstat[0])

                def scores(it):
                    b = it % 2
                    fill_S(b)
                    if it >= 8:
                        pe.wait_ge(qblk_ready, 1 if l == 0 else 2 + REQ)
                    for sl in range(2):
                        o = S[:, b, sl * MT:(sl + 1) * MT]
                        if it < 8:
                            qt, hh = it // 2, 2 * (it % 2) + sl
                            m = mm(o, xq[:, hh, qt * P:(qt + 1) * P], mkT[:, l, hh, :], True, True)
                            continue
                        pair = 2 * (it - 8) + sl
                        pe.wait_ge(xcache_in[pair], 32 * (l + 1))
                        for e in range(2):
                            for hh in range(MH):
                                m = mm(o[64 * e:64 * e + 64, :], xqb[:, 2 * pair + e, hh * 64:(hh + 1) * 64],
                                       xkc[:, pair, e, hh, :], hh == 0, hh == MH - 1)
                    m.then_inc(S_done, 1)

                def transposes(it):
                    b = it % 2
                    fill_Q(b)
                    pe.wait_ge(prob_ready, (NX + NFOX) * l + it + 1)
                    for k in range(4):
                        m = nc.tensor.transpose(Q[:, b, k * P:(k + 1) * P],
                                                xP[:, it % 3, k // 2, k % 2 * P:(k % 2 + 1) * P], ident)
                    m.then_inc(Q_done, 1)

                def values(it):
                    b = it % 2
                    out = begin(TILE0[f"xo{l}"] + it)
                    pe.wait_ge(Q_read[b], nQ[b])
                    for sl in range(2):
                        if it < 8:
                            hh = 2 * (it % 2) + sl
                            for kh in range(2):
                                m = mm(out[:, sl * P:(sl + 1) * P], mv[:, l, kh, hh * P:(hh + 1) * P],
                                       xPT[:, b, 2 * sl + kh, :], kh == 0, kh == 1)
                            continue
                        pair = 2 * (it - 8) + sl
                        for e in range(2):
                            for hh in range(MH):
                                at = e * 64 + hh * STEP
                                for kh in range(2):
                                    m = mm(out[:, sl * P + at:sl * P + at + STEP],
                                           xvc[:, pair, e, kh, hh * P:(hh + 1) * P],
                                           xPT[:, b, 2 * sl + kh, at:at + STEP], kh == 0, kh == 1)
                    m.then_inc(tile_done, 1)

                for it in range(NX + 3):
                    if it < NX:
                        scores(it)
                    if 2 <= it <= NX + 1:
                        transposes(it - 2)
                    if it >= 3:
                        values(it - 3)
                read_wait(pe, TILE0[f"xo{l}"] + NX - 2)
                read_wait(pe, TILE0[f"xo{l}"] + NX - 1)
                projections(f"wo{l}", 8, 4, rows(xo))
                residual_stat(3 * l + 1)
                for half in "ab":
                    t0, p0 = TILE0[f"up{l}{half}"], PIECE0[f"up{l}{half}"]
                    first = APPLIED[f"ffn{l}"] - KD + 1 if half == "a" else None
                    for j in range(2):
                        split_product(t0 + j, j, p0 + j, KD, hs, normed=first if j == 0 else None)
                    with pe.Fori(1, HALF) as i:
                        for j in range(2):
                            split_product(t0 + j, j, i * 2 + (p0 + j), KD, hs, before=i + (t0 + j) // 2)
                    t0, p0 = TILE0[f"down{l}{half}"], PIECE0[f"down{l}{half}"]
                    read_wait(pe, t0 - 2 * HALF + 2 * KS - 1)
                    def down(j, i=0, before=None):
                        n, p = t0 + j, i * 4 + (p0 + 2 * j)
                        split_product(n, 0, p, KS, gs, before=before, stop=False)
                        read_wait(pe, t0 - 1)
                        split_product(n, 1, p + 1, HALF - KS, gs, start=KS)

                    with pe.Fori(0, KD // 2) as i:
                        for j in range(2):
                            down(j, i, before=i + (t0 + j) // 2)
                if l == 0:
                    residual_stat(2)

            pe.wait_ge(mixed, 4)
            pe.wait_ge(applied, APPLIED["gn1"])
            projections("evout", 8, KD, rows(h))
            cross_and_ffn(0)
            narrow("f", "wf", APPLIED["mix1"] - KD + 1)
            sa, sc = chunk(CHUNK["fv"]), chunk(CHUNK["fv"] + 1)
            for c in range(NCH):
                frame_major(TILE0["fv"] + c, lambda k: h[:, k, c * P:(c + 1) * P], sa, sc)
            pe.wait_ge(h1_split, KD)
            t0, p0 = TILE0["cgu"], PIECE0["cgu"]
            with pe.Fori(0, 6) as i:
                for j in range(2):
                    split_product(t0 + j, j, i * 2 + (p0 + j), KD, hs1, ws1, before=i + (t0 + j) // 2)
            t0, p0 = TILE0["fqk"], PIECE0["fqk"]
            for j in range(8):
                split_product(t0 + j, j % 2, p0 + j, KD, hs1, ws1)
                if j:
                    stat(0, 1, cst("half"))
            stat(0, 1, cst("half"))
            pe.wait_ge(applied, APPLIED["fqk.7"])
            pe.wait_ge(fcum_ready, 1)
            pe.wait_ge(stat_read, nstat[0])
            nd16 = cst("nd16", NH)

            def fox_scores(it):
                b = it % 2
                fill_S(b)
                if it < 4 * NH:
                    hh, qt = FOX_ITEMS[it]
                    e, j, w = hh % 2, hh // 2, (qt + 1) * P
                    o, fr = S[:, b, 0:w], slice(qt * P, (qt + 1) * P)
                    mm(o, fqk[64 * e:64 * e + 64, j, fr], fqk[64 * e:64 * e + 64, 4 + j, 0:w], True, False,
                       skip_group_check=True)
                    if qt == 0:
                        pe.wait_ge(fdif_ready, hh + 1)
                    mm(o, fdif[:, hh % 2, 0, fr], fdif[:, hh % 2, 1, 0:w], False, False, skip_group_check=True)
                    m = mm(S[:, b, qt * P:w], ident, cst("cmask"), False, True, skip_group_check=True)
                else:
                    rq = it - 4 * NH
                    old, new = S[:, b, 0:PAST], S[:, b, PAST:PAST + P]
                    pe.wait_ge(qblk_ready, 1 + rq + 1)
                    pe.wait_ge(keys_in[rq % 2], 16 * (rq // 2 + 1))
                    for j in range(4):
                        w = qblk[:, rq % 2, j * P:(j + 1) * P]
                        mm(old, w, kc[:, rq % 2, j, :], j == 0, False, skip_group_check=True)
                        mm(new, w, fqk[:, 4 + j, SEQ:T], False, False, skip_group_check=True)
                    mm(S[:, b, 0:384], fqd[:, rq % 2, :, :].rearrange("p a b -> p (a b)"),
                       ones[0:NH, 0:1].broadcast_to([NH, 384]), False, False, skip_group_check=True)
                    mm(old, nd16, fcr[:, rq, 0:PAST], False, False, skip_group_check=True)
                    mm(new, nd16, fcr[:, :, PAST:KALL], False, False, skip_group_check=True)
                    o = CONST["negwin"][0] + (REQ - 1 - rq) * STEP
                    mm(new, ones[0:1, :], const[0:1, o:o + P], False, False, skip_group_check=True)
                    m = mm(new[:, rq * STEP:(rq + 1) * STEP], cst("r16", STEP), cst("m16", STEP), False, True,
                           skip_group_check=True)
                m.then_inc(S_done, 1)

            def fox_tiles(it):
                return FOX_ITEMS[it][1] + 1 if it < 4 * NH else 3

            def fox_transposes(it):
                b = it % 2
                fill_Q(b)
                pe.wait_ge(prob_ready, NX + it + 1)
                for k in range(fox_tiles(it)):
                    m = nc.tensor.transpose(Q[:, b, k * P:(k + 1) * P], fP[:, it % 3, k * P:(k + 1) * P], ident)
                m.then_inc(Q_done, 1)

            def fox_values(it):
                b = it % 2
                out = begin(TILE0["fo"] + it)
                pe.wait_ge(Q_read[b], nQ[b])
                kt = fox_tiles(it)
                if it < 4 * NH:
                    hh = FOX_ITEMS[it][0]
                    e = hh % 2
                    for k in range(kt):
                        m = mm(out[64 * e:64 * e + 64, 0:P], fv[:, k, hh * HD:(hh + 1) * HD], fPT[:, b, k, :],
                               k == 0, k == kt - 1)
                else:
                    rq = it - 4 * NH
                    pe.wait_ge(values_in[rq % 2], 16 * (rq // 2 + 1))
                    for j in range(4):
                        for k in range(kt):
                            v = vc[:, rq % 2, k, j * P:(j + 1) * P] if k < 2 else fv[:, 4, j * P:(j + 1) * P]
                            m = mm(out[:, j * 32:(j + 1) * 32], v, fPT[:, b, k, j * 32:(j + 1) * 32],
                                   k == 0, k == kt - 1)
                m.then_inc(tile_done, 1)

            for it in range(NFOX + 3):
                if it < NFOX:
                    fox_scores(it)
                if 2 <= it <= NFOX + 1:
                    fox_transposes(it - 2)
                if it >= 3:
                    fox_values(it - 3)
            read_wait(pe, TILE0["fo"] + NFOX - 2)
            read_wait(pe, TILE0["fo"] + NFOX - 1)
            projections("odout", 8, KD, rows(h))
            cross_and_ffn(1)

        @block.scalar
        def _(act):
            nsq, nsum, nstat, nself = [0], [0], [0], [0]

            def A(*a, **k):
                return nc.scalar.activation(*a, **k)

            def own(ins):
                ins.then_inc(act_self, 1)
                nself[0] += 1
                act.wait_ge(act_self, nself[0])

            def square(src, width=T):
                if nsq[0] >= 2:
                    act.wait_ge(sq_used, SUMMED[nsq[0] - 2])
                A(sq[:, nsq[0] % 2, 0:width], src, ACT.Square).then_inc(sq_ready, 1)
                nsq[0] += 1

            def sums(tiles):
                nsum[0] += tiles
                act.wait_ge(sq_used, nsum[0])
                m = nstat[0]
                if m >= 2:
                    by_pool, count = NORM[m - 2]
                    act.wait_ge(mk_applied if by_pool else applied, count)
                nstat[0] += 1
                return rstd[:, m % 2, :]

            def inv_std(tiles, scale, eps=0, width=T):
                r = sums(tiles)[:, 0:width]
                A(r, QF[:, 0:width], ACT.Ln, scale=scale, bias=small[:, eps:eps + 1]).then_inc(stat_read, 1)
                act.wait_ge(stat_read, nstat[0])
                A(r, r, ACT.Exp, scale=-0.5).then_inc(rstd_ready, 1)

            def residual_inv_std(tiles):
                A(small[:, 5:6], small[:, 2:3], ACT.Ln)
                inv_std(tiles, 1.0 / D)

            def evacuate(dst, n, func=ACT.Copy, width=T, out=G):
                tile_wait(act, n)
                A(dst, out[n % 2][:, 0:width], func).then_inc(read[n % 2], 1)

            def head_norms(dst, n0, tiles, scale, width=T, out=G, after=None):
                for j in range(tiles):
                    evacuate(dst(j), n0 + j, width=width, out=out)
                    if after:
                        after(j)
                    read_wait(act, n0 + j)
                    square(dst(j), width)
                    if j:
                        inv_std(1, scale, width=width)
                inv_std(1, scale, width=width)

            def high_part(name, u, s, done, count, i=0):
                c = CHUNK[name] + u
                if s == 0:
                    act.wait_ge(chunk_in[c % RING], i * 16 + 16 * (c // RING + 1))
                act.wait_ge(done, count)
                src, hi, _ = piece(name, u, s)
                A(hi, src, ACT.Copy).then_inc(high, 1)

            def residual_square(norms, n, j):
                read_wait(act, n)
                if j < 2:
                    square(x[:, j, :])
                else:
                    act.wait_ge(added, SUM_ADDS * norms + max(1, j - 2))
                    A(sq[:, nsq[0] % 2, :], x[:, j, :], ACT.Square).then_inc(sq_ready, 1)
                    nsq[0] += 1

            def residual_squares(norms, name, after=None):
                for j in range(KD):
                    residual_square(norms, TILE0[name] + j, j)
                    if after:
                        after(j)
                residual_inv_std(2)

            act.wait_ge(small_ready, 1)
            for k in range(KD):
                act.wait_ge(x_in[k // 2], 16)
                square(x[:, k, :])
            residual_inv_std(KD)
            t0 = TILE0["glu"]
            for j in range(4):
                if j >= 2:
                    read_wait(act, t0 + 2 * (j - 2) + 1)
                evacuate(tmp[:, j % 2, :], t0 + 2 * j, ACT.Sigmoid)
                if j == 0:
                    act.wait_ge(mem_in, 16)
                    for k in range(KD):
                        square(memx[:, k, :], MT)
                    inv_std(KD, 1.0 / D, width=MT)
            for l in range(LAYERS):
                head_norms(lambda j: mkT[:, l, j, :], TILE0[f"mk{l}"], 4, 1.0 / P, MT)
                for m2 in range(2):
                    evacuate(mv[:, l, m2, :], TILE0[f"mv{l}"] + m2, width=512)
            act.wait_ge(par_in, 16)
            for j in range(KD):
                n = TILE0["xbc"] + j
                tile_wait(act, n)
                a, b = padded(xbcp, j, XW - 1, XPROMPT, XREQ, XW - 1)
                A(a, G[n % 2][:, 0:SEQ], ACT.Copy)
                A(b, runs(G[n % 2][:, SEQ:T]), ACT.Copy).then_inc(read[n % 2], 1)
            for j in range(KD):
                act.wait_ge(xconv, 2 * XW * (j + 1))
                A(xbcc[:, j, :], tmp[:, j % 2, :], ACT.Silu).then_inc(xbc_done, 1)
            act.wait_ge(dt_abs, 1)
            own(A(dtb[:, 2, :], dtb[:, 2, :], ACT.Exp, scale=-1.0))
            A(small[0:NH, 3:4], pr("alog", 0, NH), ACT.Exp)
            A(dtb[:, 2, :], dtb[:, 2, :], ACT.Ln, bias=small[0:NH, 2:3]).then_inc(dt_log, 1)
            act.wait_ge(applied, APPLIED["mem"])
            for j in range(4):
                evacuate(zs[:, j, :], TILE0["z"] + j, ACT.Silu)
            r = sums(4)
            A(r, QF[:, 0:T], ACT.Copy).then_inc(stat_read, 1)
            act.wait_ge(stat_read, nstat[0])
            A(r, r, ACT.Copy, scale=1.0 / CONF).then_inc(rstd_ready, 1)
            act.wait_ge(cs_ready, 1)
            A(dtb[:, 2, :], dtb[:, 2, :], ACT.Exp, scale=-1.0).then_inc(de_ready, 1)
            n = TILE0["tok"] + 1
            tile_wait(act, n)
            A(decay[:, :, :].rearrange("p a b -> p (a b)"), G[n % 2][:, 0:NSEG * NH], ACT.Exp)\
                .then_inc(read[n % 2], 1)
            act.wait_ge(applied, APPLIED["mean"])
            for k in range(4):
                square(acc[:, k, :])
            inv_std(4, 1.0 / CONF, eps=1)
            act.wait_ge(applied, APPLIED["var"])
            for k in range(4):
                A(h[:, k, :], acc[:, k, :], ACT.Silu, scale=pr("lng", k), bias=pr("lnb", k)).then_inc(mixed, 1)
            act.wait_ge(outs, 16 * CONV_OUTS)
            n = TILE0["scan"]
            for c in range(NCH):
                if c < NCH - 1:
                    tile_wait(act, n + 1)
                    A(btok, G[(n + 1) % 2][:, 0:256], ACT.Copy).then_inc(read[(n + 1) % 2], 1)
                act.wait_ge(Q_read[0], c)
                for gr in range(2):
                    act.wait_ge(S_done, 2 * c + gr + 1)
                    A(Lm[:, 4 * gr:4 * gr + 4, :].rearrange("p a b -> p (a b)"), S[:, gr, :], ACT.Exp)\
                        .then_inc(S_read[gr], 1)
                if c:
                    read_wait(act, n - 2)
                elif c == 0:
                    act.wait_ge(mixed, 4)
                act.wait_ge(Q_done, 2 * c + 2)
                A(Ee.rearrange("p a b -> p (a b)"), Q[:, 1, :], ACT.Exp).then_inc(Q_read[1], 1)
                n += 5
            act.wait_ge(gated, NCH)
            for gr in range(2):
                for k in range(2):
                    square(h[:, 4 + 2 * gr + k, :])
                inv_std(2, 1.0 / 256)

            def cross_and_ffn(l):
                act.wait_ge(outs, 16 * (ODD_OUTS if l else SCAN_OUTS))
                head_norms(lambda j: xq[:, j, :], TILE0[f"q{l}"], 4, 1.0 / P)
                first = (NX + NFOX) * l

                def exps(it):
                    b, i = it % 2, first + it
                    act.wait_ge(neg_ready, i + 1)
                    act.wait_ge(Q_done, 2 * NCH + i - 2)
                    for sl in range(2):
                        m = A(xP[:, it % 3, sl, :], S[:, b, sl * MT:(sl + 1) * MT], ACT.Exp, scale=SCALE_X,
                              bias=stats[:, b, 2 + sl:3 + sl], accum_out=stats[:, b, 4 + sl:5 + sl])
                    m.then_inc(S_read[b], 1)

                def turned(it):
                    b, i = it % 2, first + it
                    act.wait_ge(Q_done, 2 * NCH + i + 1)
                    if it >= 2:
                        tile_wait(act, TILE0[f"xo{l}"] + it - 2)
                    A(xPT[:, b, :, :].rearrange("p a b -> p (a b)"), Q[:, b, :], ACT.Copy)\
                        .then_inc(Q_read[b], 1)

                for it in range(NX + 2):
                    if it < NX:
                        exps(it)
                    if it >= 2:
                        turned(it - 2)
                residual_squares(3 * l + 1, f"wo{l}", lambda j: j == 5 and [
                    high_part(f"up{l}a", 0, s, tile_done, TILE0[f"wo{l}"] + 1) for s in range(2)])
                for k in range(KD):
                    act.wait_ge(h_raw, KD * l + k + 1)
                    A(hs[:, 0, k, :], raw_tile(k), ACT.Copy).then_inc(h_hi, 1)

                def gate(j, n, step=0):
                    act.wait_ge(read[(n + 1) % 2], step * RING + (n - 3) // 2 + 1)
                    act.wait_ge(tile_done, step * (2 * RING) + n + 1)
                    A(tmp[:, j % 2, :], GF[n % 2], ACT.Silu).then_inc(read[n % 2], 1)

                for half in "ab":
                    up, down = f"up{l}{half}", f"down{l}{half}"
                    t0 = TILE0[up]

                    def tiles(u, i=0):
                        for s in range(2):
                            n = t0 + 2 * u + s
                            if s == 0:
                                gate(u, n, i)
                            nxt = (up, u + 1) if u < HALF - 1 else (down, 0)
                            high_part(*nxt, s, tile_done, i * (2 * RING) + n + 1, i)

                    with act.Fori(0, HALF // RING) as i:
                        for u in range(RING):
                            tiles(u, i)
                    for u in range(HALF // RING * RING, HALF):
                        tiles(u)
                    for j in range(KD):
                        nxt = (down, j + 1) if j < KD - 1 else (f"up{l}b", 0)
                        if j < KD - 1 or half == "a":
                            high_part(*nxt, 0, half_used, KD * (2 * l + (half == "b")) + j + 1)
                            high_part(*nxt, 1, tile_done, TILE0[down] + j + 1)
                        if l == 0 and half == "b":
                            residual_square(2, TILE0[down] + j, j)

            residual_squares(0, "evout")
            cross_and_ffn(0)
            residual_inv_std(2)
            for k in range(KD):
                act.wait_ge(applied, APPLIED["mix1"] - KD + k + 1)
                A(hs1[:, 0, k, :], h[:, k, :], ACT.Copy).then_inc(h1_hi, 1)

            t0 = TILE0["cgu"]

            def high_part1(q):
                if q < len(PIECES1):
                    high_part(*PIECES1[q], tile_done, t0 + max(0, q - 1))

            for q in range(2):
                name, u, s = PIECES1[q]
                high_part(name, u, s, tile_done, TILE0["down0b"] + KD)
            act.wait_ge(f_abs, 1)
            own(A(fx, fx, ACT.Exp, scale=-1.0))
            A(fx, fx, ACT.Ln, bias=small[0:NH, 2:3]).then_inc(f_log, 1)
            for c in range(NCH):
                evacuate(fv[:, c, :], TILE0["fv"] + c, width=512)
            for j in range(4):
                if j >= 2:
                    read_wait(act, t0 + 2 * (j - 2) + 1)
                evacuate(tmp[:, j % 2, :], t0 + 2 * j, out=GF)
                high_part1(2 * j + 2)
                high_part1(2 * j + 3)
            for q in range(8, 12):
                high_part1(q + 2)
            head_norms(lambda j: fqk[:, j, :], TILE0["fqk"], 8, 1.0 / HD, out=GF,
                       after=lambda j: high_part1(14 + j))

            def fox_width(it):
                return (FOX_ITEMS[it][1] + 1) * P if it < 4 * NH else 384

            def fox_exps(it):
                b, i, w = it % 2, NX + it, fox_width(it)
                act.wait_ge(neg_ready, i + 1)
                act.wait_ge(Q_done, 2 * NCH + i - 2)
                A(fP[:, it % 3, 0:w], S[:, b, 0:w], ACT.Exp, bias=stats[:, b, 2:3],
                  accum_out=stats[:, b, 4:5]).then_inc(S_read[b], 1)

            def fox_turned(it):
                b, i, w = it % 2, NX + it, fox_width(it)
                act.wait_ge(Q_done, 2 * NCH + i + 1)
                if it >= 2:
                    tile_wait(act, TILE0["fo"] + it - 2)
                A(fPT[:, b, :, :].rearrange("p a b -> p (a b)")[:, 0:w], Q[:, b, 0:w], ACT.Copy)\
                    .then_inc(Q_read[b], 1)

            for it in range(NFOX + 2):
                if it < NFOX:
                    fox_exps(it)
                if it >= 2:
                    fox_turned(it - 2)
            residual_squares(3, "odout")
            cross_and_ffn(1)

        @block.vector
        def _(dve):
            v = nc.vector
            nself, nnorm, nadd = [0], [0], [0]

            def own(ins):
                ins.then_inc(dve_self, 1)
                nself[0] += 1
                dve.wait_ge(dve_self, nself[0])

            def norm(pairs, gain, width=T):
                m = nnorm[0]
                dve.wait_ge(rstd_ready, m + 1)
                for j, (dst, src) in enumerate(pairs):
                    v.scalar_tensor_tensor(out=dst, in0=src, scalar=gain(j), in1=rstd[:, m % 2, 0:width],
                                           op0=ALU.mult, op1=ALU.mult).then_inc(applied, 1)
                nnorm[0] += 1

            def norm_x(name):
                norm([(h[:, k, :], x[:, k, :]) for k in range(KD)], lambda k: pr(name, k))

            def add_residual(name, after=None):
                for j in range(KD):
                    n = TILE0[name] + j
                    tile_wait(dve, n)
                    v.tensor_tensor(x[:, j, :], x[:, j, :], G[n % 2][:, 0:T], ALU.add)\
                        .then_inc(read[n % 2], 1)
                    add_square(name, j)
                    if after:
                        after(j)

            def add_square(name, j):
                if j < 2:
                    return
                m = nnorm[0]
                total = rstd[:, m % 2, :]
                dve.wait_ge(sq_ready, SQUARE0[name] + j)
                if j == 2:
                    dve.wait_ge(applied, NORM[m - 2][1])
                    v.tensor_tensor(total, sq[:, 0, :], sq[:, 1, :], ALU.add).then_inc(added, 1)
                else:
                    dve.wait_ge(added, nadd[0])
                    v.tensor_tensor(total, total, sq[:, (j - 1) % 2, :], ALU.add).then_inc(added, 1)
                nadd[0] += 1

            def low_part(name, u, s, i=0):
                dve.wait_ge(high, i * (2 * RING) + (PIECE0[name] + 2 * u + s + 1))
                src, hi, lo = piece(name, u, s)
                v.tensor_tensor(lo, src, hi.bitcast(F32), ALU.subtract).then_inc(split, 1)

            v.memset(small[:, 0:1], 1e-6)
            v.memset(small[:, 1:2], 1e-5)
            v.memset(small[:, 2:3], 1.0).then_inc(small_ready, 1)
            v.memset(aglu[:, :, 0:CW - 1], 0.0)
            v.memset(xbcp[:, :, 0:XW - 1], 0.0).then_inc(small_ready, 1)
            v.memset(hT, 0.0).then_inc(hT_zero, 1)
            dve.wait_ge(const_in, 16)
            dve.wait_ge(par_in, 16)
            for i in range(KD // 2):
                dve.wait_ge(x_in[i], 16)
            v.tensor_scalar(small[:, 4:5], pr("fq"), HD ** -0.5, None, ALU.mult)
            norm_x("mix0")
            for j in range(4):
                n = TILE0["glu"] + 2 * j
                read_wait(dve, n)
                tile_wait(dve, n + 1)
                a, b = padded(aglu, j, CW - 1, CPROMPT, CREQ, CW - 1)
                v.tensor_tensor(a, tmp[:, j % 2, 0:SEQ], G[(n + 1) % 2][:, 0:SEQ], ALU.mult)
                v.tensor_tensor(b, runs(tmp[:, j % 2, SEQ:T]), runs(G[(n + 1) % 2][:, SEQ:T]), ALU.mult)\
                    .then_inc(read[(n + 1) % 2], 1)
                if j == 0:
                    norm([(memh[:, l, k, :], memx[:, k, :]) for l in range(2) for k in range(KD)],
                         lambda i: pr(f"mem{i // KD}", i % KD), MT)
            nnorm[0] += 8
            dve.wait_ge(pads_in, 16 * 12)
            dve.wait_ge(small_ready, 2)
            read_wait(dve, TILE0["glu"] + 5)
            read_wait(dve, TILE0["glu"] + 7)
            dst = [d for j in range(4) for d in (acc[:, j, 0:SEQ], runs(acc[:, j, SEQ:T]))]
            for i, d in enumerate(dst):
                src = padded(aglu, i // 2, 0, CPROMPT, CREQ, 0)[i % 2]
                v.tensor_scalar(d, src, pr("cw", i // 2 * CW), pr("cb", i // 2), ALU.mult, ALU.add)\
                    .then_inc(conv, 1)
            with dve.Fori(1, CW) as w:
                for i, d in enumerate(dst):
                    j = i // 2
                    if i % 2 == 0:
                        src = aglu[:, j, bass.ds(w, SEQ)]
                    else:
                        src = aglu[:, j, CPROMPT:].rearrange("p (r t) -> p r t", r=REQ)[:, :, bass.ds(w, STEP)]
                    tap = par[:, bass.ds(w + (PAR["cw"][0] + j * CW), 1)]
                    dve.wait_ge(conv, w * 8 + (i - 7))
                    v.scalar_tensor_tensor(out=d, in0=src, scalar=tap, in1=d, op0=ALU.mult, op1=ALU.add)\
                        .then_inc(conv, 1)
            done = 0
            for j in range(KD):
                read_wait(dve, TILE0["xbc"] + j)
                if j >= 2:
                    dve.wait_ge(xbc_done, j - 1)
                out = (tmp[:, j % 2, 0:SEQ], runs(tmp[:, j % 2, SEQ:T]))
                for w in range(XW):
                    for i in range(2):
                        src = padded(xbcp, j, 0, XPROMPT, XREQ, w)[i]
                        if w == 0:
                            ins = v.tensor_scalar(out[i], src, pr("xw", j * XW), pr("xb", j), ALU.mult, ALU.add)
                        else:
                            dve.wait_ge(xconv, done - 1)
                            ins = v.scalar_tensor_tensor(out=out[i], in0=src, scalar=pr("xw", j * XW + w),
                                                         in1=out[i], op0=ALU.mult, op1=ALU.add)
                        ins.then_inc(xconv, 1)
                        done += 1
            n = TILE0["dt"]
            tile_wait(dve, n)
            v.tensor_scalar(dtb[:, 1, :], G[n % 2][0:NH, 0:T], pr("dtb", 0, NH), None, ALU.add)\
                .then_inc(read[n % 2], 1)
            read_wait(dve, n)
            v.scalar_tensor_tensor(out=dtb[:, 2, :], in0=dtb[:, 1, :], scalar=-1.0, in1=dtb[:, 1, :],
                                   op0=ALU.mult, op1=ALU.max).then_inc(dt_abs, 1)
            dve.wait_ge(dt_log, 1)
            own(v.scalar_tensor_tensor(out=dtb[:, 1, :], in0=dtb[:, 1, :], scalar=0.0, in1=dtb[:, 2, :],
                                       op0=ALU.max, op1=ALU.add))
            own(v.tensor_scalar(dtb[:, 0, :], dtb[:, 1, :], small[0:NH, 3:4], -1.0, ALU.mult, ALU.mult))
            segments = [(c * P, P) for c in range(4)] + [(SEQ + q * STEP, STEP) for q in range(REQ)]
            one = cst("ones", NH)[:, 0:1]
            for at, w in segments:
                ins = v.tensor_tensor_scan(out=dtb[:, 3, at:at + w], data0=one.broadcast_to([NH, w]), data1=dtb[:, 0, at:at + w],
                                           initial=0.0, op0=ALU.mult, op1=ALU.add)
            own(ins)
            v.tensor_scalar(dtb[:, 0, :], dtb[:, 3, :], -1.0, None, ALU.mult)
            v.tensor_copy(csend[:, 0:4], dtb[:, 3, P - 1:SEQ:P])
            own(v.tensor_copy(csend[:, 4:NSEG], dtb[:, 3, SEQ + STEP - 1:T:STEP]))
            v.tensor_tensor(cdiag[:, :, :], csend[:, :].unsqueeze(2).broadcast_to([NH, NSEG, NH]),
                            cst("d8", NH).unsqueeze(1).broadcast_to([NH, NSEG, NH]), ALU.mult)
            for at, w, s0, ns in ((0, P, 0, 4), (SEQ, STEP, 4, REQ)):
                seg = lambda row: dtb[:, row, at:at + w * ns].rearrange("p (s t) -> p s t", s=ns)
                ins = v.tensor_tensor(seg(2), seg(3), csend[:, s0:s0 + ns].unsqueeze(2).broadcast_to([NH, ns, w]),
                                      ALU.subtract)
            ins.then_inc(cs_ready, 1)
            m = nnorm[0]
            dve.wait_ge(rstd_ready, m + 1)
            for k in range(4):
                v.tensor_tensor(acc[:, k, :], acc[:, k, :], rstd[:, m % 2, :], ALU.subtract).then_inc(applied, 1)
            n = TILE0["tok"]
            tile_wait(dve, n)
            v.tensor_copy(toks[:, :, :, :].rearrange("p a b c -> p (a b c)"), G[n % 2][:, 0:2 * NCH * NH])\
                .then_inc(read[n % 2], 1)
            dve.wait_ge(rstd_ready, m + 2)
            for k in range(4):
                v.tensor_tensor(acc[:, k, :], acc[:, k, :], rstd[:, (m + 1) % 2, :], ALU.mult).then_inc(applied, 1)
            nnorm[0] += 2
            read_wait(dve, n)
            read_wait(dve, n + 1)
            dve.wait_ge(outs, 16 * CONV_OUTS)
            n = TILE0["scan"]
            for c in range(NCH):
                fr = slice(c * P, (c + 1) * P)
                run = c == NCH - 1
                heads = lambda ap: ap.rearrange("p (h d) -> p h d", d=HD)
                tile_wait(dve, n)
                v.tensor_tensor(heads(xdt), heads(G[n % 2][:, 0:512]),
                                toks[:, 0, c, :].unsqueeze(2).broadcast_to([P, NH, HD]), ALU.mult)\
                    .then_inc(read[n % 2], 1)
                read_wait(dve, n)
                v.tensor_tensor(heads(xdte), heads(xdt), toks[:, 1, c, :].unsqueeze(2).broadcast_to([P, NH, HD]),
                                ALU.mult).then_inc(xdte_ready, 1)
                if run:
                    tile_wait(dve, n + 1)
                    v.tensor_tensor(bmask, G[(n + 1) % 2][:, 0:256].unsqueeze(1).broadcast_to([P, REQ, 256]),
                                    cst("req").unsqueeze(2).broadcast_to([P, REQ, 256]), ALU.mult)\
                        .then_inc(read[(n + 1) % 2], 1)
                dve.wait_ge(Q_done, 2 * c + 1)
                if c == 0:
                    dve.wait_ge(mixed, 4)
                for gr in range(2):
                    dve.wait_ge(S_read[gr], c + 1)
                    ins = v.tensor_tensor(Pm[:, 4 * gr:4 * gr + 4, :], Lm[:, 4 * gr:4 * gr + 4, :],
                                          Q[:, 0, gr * P:(gr + 1) * P].unsqueeze(1).broadcast_to([P, 4, P]),
                                          ALU.mult)
                ins.then_inc(Q_read[0], 1)
                tile_wait(dve, n + 3)
                dve.wait_ge(Q_read[1], c + 1)
                four = lambda n: G[n % 2][:, 0:512].rearrange("p (j l) -> p j l", j=4)
                v.tensor_tensor(ysc, four(n + 3), Ee, ALU.mult).then_inc(read[(n + 3) % 2], 1)
                read_wait(dve, n + 3)
                v.tensor_tensor(ysc, ysc, four(n + 2), ALU.add).then_inc(read[(n + 2) % 2], 1)
                if run:
                    own(v.tensor_tensor(h0T.rearrange("p r (h d) -> p (r h) d", d=HD),
                                        h0T.rearrange("p r (h d) -> p (r h) d", d=HD),
                                        decay[:, 4:NSEG, :].rearrange("p r h -> p (r h)").unsqueeze(2)
                                        .broadcast_to([P, REQ * NH, HD]), ALU.mult))
                else:
                    own(v.tensor_tensor(heads(hT), heads(hT),
                                        decay[:, c, :].unsqueeze(2).broadcast_to([P, NH, HD]), ALU.mult))
                for k in range(REQ if run else 1):
                    tile_wait(dve, n + 4 + k)
                    st = h0T[:, k, :] if run else hT
                    v.tensor_tensor(st, st, G[(n + 4 + k) % 2][:, 0:512], ALU.add)\
                        .then_inc(read[(n + 4 + k) % 2], 1)
                read_wait(dve, n + 2)
                for j in range(4):
                    ins = v.scalar_tensor_tensor(out=h[:, 4 + j, fr], in0=xbcc[:, j, fr], scalar=pr("dskip", j),
                                                 in1=ysc[:, j, :], op0=ALU.mult, op1=ALU.add)
                own(ins)
                v.tensor_tensor(h[:, 4:8, fr], h[:, 4:8, fr], zs[:, :, fr], ALU.mult).then_inc(gated, 1)
                n += 5
            dve.wait_ge(gated, NCH)
            for gr in range(2):
                norm([(h[:, 4 + 2 * gr + k, :],) * 2 for k in range(2)], lambda k: pr("gn", 2 * gr + k))

            def cross_and_ffn(l):
                norm_x(f"cross{l}")
                dve.wait_ge(outs, 16 * (ODD_OUTS if l else SCAN_OUTS))
                own(v.memset(xqb, 0.0))
                for j in range(4):
                    norm([(xq[:, j, :],) * 2], lambda _: pr(f"xq{l}"))
                dve.wait_ge(applied, APPLIED[f"q{l}.3"])
                for hh in range(MH):
                    ins = v.tensor_copy(xqb[:, :, hh * 80:hh * 80 + STEP], runs(xq[:, hh, SEQ:T]))
                ins.then_inc(qblk_ready, 1)
                first = (NX + NFOX) * l

                def maxima(it):
                    b, i = it % 2, first + it
                    dve.wait_ge(S_done, 2 * NCH + i + 1)
                    own(v.tensor_reduce(stats[:, b, 0:2], S[:, b, :].rearrange("p (s m) -> p s m", s=2),
                                        AX_X, ALU.max))
                    v.tensor_scalar(stats[:, b, 2:4], stats[:, b, 0:2], -SCALE_X, None, ALU.mult)\
                        .then_inc(neg_ready, 1)

                def normalise(it):
                    b, i = it % 2, first + it
                    dve.wait_ge(S_read[b], NCH + i // 2 + 1)
                    own(v.reciprocal(stats[:, b, 6:8], stats[:, b, 4:6]))
                    v.tensor_tensor(xP[:, it % 3, :, :], xP[:, it % 3, :, :],
                                    stats[:, b, 6:8].unsqueeze(2).broadcast_to([P, 2, MT]), ALU.mult)\
                        .then_inc(prob_ready, 1)

                def results(it):
                    n = TILE0[f"xo{l}"] + it
                    tile_wait(dve, n)
                    o = G[n % 2]
                    if it < 8:
                        qt, hh = it // 2, 2 * (it % 2)
                        ins = v.tensor_copy(xo[:, hh:hh + 2, qt * P:(qt + 1) * P],
                                            o[:, 0:2 * P].rearrange("p (s q) -> p s q", s=2))
                    else:
                        for sl in range(2):
                            at = SEQ + (2 * (it - 8) + sl) * 2 * STEP
                            for e in range(2):
                                src = o[:, sl * P + e * 64:sl * P + e * 64 + 64]
                                ins = v.tensor_copy(xo[:, :, at + e * STEP:at + (e + 1) * STEP],
                                                    src.rearrange("p (h t) -> p h t", h=MH))
                    ins.then_inc(read[n % 2], 1)

                for it in range(NX + 3):
                    if it < NX:
                        maxima(it)
                    if 1 <= it <= NX:
                        normalise(it - 1)
                    if it >= 3:
                        results(it - 3)
                add_residual(f"wo{l}", lambda j: j == 5 and [low_part(f"up{l}a", 0, s) for s in range(2)])
                m = nnorm[0]
                dve.wait_ge(rstd_ready, m + 1)
                for k in range(KD + 1):
                    if k < KD:
                        if k >= 4:
                            dve.wait_ge(applied, APPLIED[f"ffn{l}"] - KD + k - 3)
                        v.scalar_tensor_tensor(out=raw_tile(k), in0=x[:, k, :], scalar=pr(f"ffn{l}", k),
                                               in1=rstd[:, m % 2, :], op0=ALU.mult, op1=ALU.mult).then_inc(h_raw, 1)
                    if k:
                        dve.wait_ge(h_hi, KD * l + k)
                        v.tensor_tensor(hs[:, 1, k - 1, :], raw_tile(k - 1), hs[:, 0, k - 1, :].bitcast(F32),
                                        ALU.subtract).then_inc(applied, 1)
                nnorm[0] += 1
                gf = gs[:, :, :, :].rearrange("p a k t -> p a (k t)")

                def gated_tile(j, n, step=0):
                    at = bass.ds(step * (RING * T) + j * T, T)
                    raw, hi, lo = tmp[:, j % 2, :], gf[:, 0, at], gf[:, 1, at]
                    own = step * (2 * RING) + (nself[0] + 2 * j)
                    dve.wait_ge(read[n % 2], step * RING + n // 2 + 1)
                    dve.wait_ge(tile_done, step * (2 * RING) + n + 2)
                    v.tensor_tensor(raw, raw, GF[(n + 1) % 2], ALU.mult).then_inc(dve_self, 1)
                    dve.wait_ge(dve_self, own + 1)
                    v.tensor_copy(hi, raw).then_inc(dve_self, 1)
                    dve.wait_ge(dve_self, own + 2)
                    v.tensor_tensor(lo, raw, hi.bitcast(F32), ALU.subtract).then_inc(read[(n + 1) % 2], 1)

                for half in "ab":
                    up, down = f"up{l}{half}", f"down{l}{half}"
                    t0 = TILE0[up]

                    def tiles(u, i=0):
                        nxt = (up, u + 1) if u < HALF - 1 else (down, 0)
                        low_part(*nxt, 0, i)
                        gated_tile(u, t0 + 2 * u, i)
                        low_part(*nxt, 1, i)

                    with dve.Fori(0, HALF // RING) as i:
                        for u in range(RING):
                            tiles(u, i)
                    for u in range(HALF // RING * RING, HALF):
                        tiles(u)
                    nself[0] += 2 * HALF
                    for j in range(KD):
                        n = TILE0[down] + j
                        nxt = (down, j + 1) if j < KD - 1 else (f"up{l}b", 0)
                        split_next = j < KD - 1 or half == "a"
                        if split_next:
                            low_part(*nxt, 0)
                        tile_wait(dve, n)
                        v.tensor_tensor(x[:, j, :], x[:, j, :], GF[n % 2], ALU.add).then_inc(read[n % 2], 1)
                        if l == 0 and half == "b":
                            add_square(down, j)
                        if split_next:
                            low_part(*nxt, 1)

            add_residual("evout")
            cross_and_ffn(0)
            norm_x("mix1")
            n = TILE0["f"]
            tile_wait(dve, n)
            v.tensor_scalar(fl, G[n % 2][0:NH, 0:T], pr("fb", 0, NH), None, ALU.add).then_inc(read[n % 2], 1)
            read_wait(dve, n)
            v.scalar_tensor_tensor(out=fx, in0=fl, scalar=-1.0, in1=fl, op0=ALU.mult, op1=ALU.max)\
                .then_inc(f_abs, 1)
            dve.wait_ge(f_log, 1)
            v.scalar_tensor_tensor(out=fl, in0=fl, scalar=0.0, in1=fx, op0=ALU.min, op1=ALU.subtract)\
                .then_inc(f_ready, 1)
            dve.wait_ge(f_ready, 1)
            own(v.tensor_tensor_scan(out=fcp, data0=one.broadcast_to([NH, SEQ]), data1=fl[:, 0:SEQ], initial=0.0,
                                     op0=ALU.mult, op1=ALU.add))
            taps = [0]

            def short_conv(j):
                dve.wait_ge(sc_in, 16 * 4)
                read_wait(dve, TILE0["cgu"] + 2 * j + 1)
                for w in range(SW):
                    for i in range(2):
                        out = (cacc[:, j, 0:SEQ], runs(cacc[:, j, SEQ:T]))[i]
                        src = padded(cgu, j, 0, SPROMPT, SREQ, w)[i]
                        if w == 0:
                            ins = v.tensor_scalar(out, src, pr("sw", j * SW), None, ALU.mult)
                        else:
                            dve.wait_ge(gbc, taps[0] - 1)
                            ins = v.scalar_tensor_tensor(out=out, in0=src, scalar=pr("sw", j * SW + w), in1=out,
                                                         op0=ALU.mult, op1=ALU.add)
                        ins.then_inc(gbc, 1)
                        taps[0] += 1

            for j in range(4):
                n = TILE0["cgu"] + 2 * j
                read_wait(dve, n)
                tile_wait(dve, n + 1)
                if j == 0:
                    v.memset(cgu[:, :, 0:SW - 1], 0.0)
                a, b = padded(cgu, j, SW - 1, SPROMPT, SREQ, SW - 1)
                v.tensor_tensor(a, tmp[:, j % 2, 0:SEQ], GF[(n + 1) % 2][:, 0:SEQ], ALU.mult)
                v.tensor_tensor(b, runs(tmp[:, j % 2, SEQ:T]), runs(GF[(n + 1) % 2][:, SEQ:T]), ALU.mult)\
                    .then_inc(read[(n + 1) % 2], 1)
                if j:
                    short_conv(j - 1)
            short_conv(3)
            dve.wait_ge(gbc, taps[0])
            for j in range(4):
                n = TILE0["gb"] + j
                tile_wait(dve, n)
                v.tensor_tensor(cacc[:, j, :], cacc[:, j, :], GF[n % 2], ALU.mult).then_inc(read[n % 2], 1)
            for j in range(8):
                norm([(fqk[:, j, :],) * 2], lambda _: small[:, 4:5] if j < 4 else pr("fk"))
            own(v.memset(fdif, 0.0))
            v.memset(fdif[32:BR, :, 0, :], -1.0)
            v.memset(fdif[0:NH, :, 1, :], 1.0).then_inc(fcum_ready, 1)

            def head_factors(hh):
                one_hot = cst("d8", NH)[:, hh:hh + 1]
                v.tensor_scalar(fdif[0:NH, hh % 2, 0, :], fcp, one_hot, None, ALU.mult)
                v.tensor_scalar(fdif[32:BR, hh % 2, 1, :], fcp, one_hot, None, ALU.mult).then_inc(fdif_ready, 1)

            def request_sums():
                v.memset(qblk, 0.0)
                dve.wait_ge(flog_in, 16)
                own(v.tensor_copy(flog[:, :, PAST:KALL], runs(fl[:, SEQ:T])))
                for rq in range(REQ):
                    ins = v.tensor_tensor_scan(out=fcr[:, rq, :], data0=one.broadcast_to([NH, KALL]),
                                               data1=flog[:, rq, :], initial=0.0, op0=ALU.mult, op1=ALU.add)
                own(ins)

            dve.wait_ge(applied, APPLIED["fqk.7"])
            dve.wait_ge(fcum_ready, 1)
            for hh in range(2):
                head_factors(hh)

            def fox_queries(rq):
                b = rq % 2
                if rq >= 2:
                    dve.wait_ge(S_done, 2 * NCH + NX + 4 * NH + rq - 1)
                for e in range(2):
                    half = slice(64 * e, 64 * e + 64)
                    v.tensor_copy(qblk[half, b, :].rearrange("p (j s) -> p j s", s=160)
                                  [:, :, STEP * e:STEP * (e + 1)],
                                  fqk[half, 0:4, SEQ + rq * STEP:SEQ + (rq + 1) * STEP])
                v.tensor_tensor(fqd[:, b, :, :], cst("d8", NH).unsqueeze(2).broadcast_to([NH, NH, STEP]),
                                fcr[:, rq, PAST:KALL].unsqueeze(1).broadcast_to([NH, NH, STEP]), ALU.mult)\
                    .then_inc(qblk_ready, 1)

            def fox_width(it):
                return (FOX_ITEMS[it][1] + 1) * P if it < 4 * NH else 384

            def fox_maxima(it):
                b, i = it % 2, NX + it
                dve.wait_ge(S_done, 2 * NCH + i + 1)
                own(v.tensor_reduce(stats[:, b, 0:1], S[:, b, 0:fox_width(it)], AX_X, ALU.max))
                v.tensor_scalar(stats[:, b, 2:3], stats[:, b, 0:1], -1.0, None, ALU.mult).then_inc(neg_ready, 1)

            def fox_normalise(it):
                b, i, w = it % 2, NX + it, fox_width(it)
                dve.wait_ge(S_read[b], NCH + i // 2 + 1)
                own(v.reciprocal(stats[:, b, 6:7], stats[:, b, 4:5]))
                v.tensor_scalar(fP[:, it % 3, 0:w], fP[:, it % 3, 0:w], stats[:, b, 6:7], None, ALU.mult)\
                    .then_inc(prob_ready, 1)

            def fox_results(it):
                n = TILE0["fo"] + it
                tile_wait(dve, n)
                if it < 4 * NH:
                    hh, qt = FOX_ITEMS[it]
                    half = slice(64 * (hh % 2), 64 * (hh % 2) + 64)
                    ins = v.tensor_copy(h[half, 4 + hh // 2, qt * P:(qt + 1) * P], G[n % 2][half, 0:P])
                else:
                    at = SEQ + (it - 4 * NH) * STEP
                    for e in range(2):
                        half = slice(64 * e, 64 * e + 64)
                        ins = v.tensor_copy(h[half, 4:8, at:at + STEP],
                                            G[n % 2][half, 0:P].rearrange("p (j c) -> p j c", j=4)
                                            [:, :, STEP * e:STEP * (e + 1)])
                ins.then_inc(read[n % 2], 1)

            for it in range(NFOX + 3):
                if it == 8:
                    request_sums()
                if it == 3:
                    dve.wait_ge(outs, 16 * (SCAN_OUTS + 8))
                if 0 <= it + 1 - 4 * NH < REQ:
                    fox_queries(it + 1 - 4 * NH)
                if it < NFOX:
                    fox_maxima(it)
                if it < 4 * NH and it % 4 == 0 and 2 <= it // 4 + 1 < NH:
                    head_factors(it // 4 + 1)
                if 1 <= it <= NFOX:
                    fox_normalise(it - 1)
                if it >= 3:
                    fox_results(it - 3)
            add_residual("odout")
            cross_and_ffn(1)


def _feature_major(a):
    return a.T.reshape(-1, P, a.shape[0]).transpose(1, 0, 2)


def _cols(a):
    return a.reshape(-1, P).T


def _weights(w, width=256):
    K, N = w.shape
    return w.reshape(K // P, P, N // width, width).transpose(2, 1, 0, 3).reshape(N // width, P, -1)


def _paired(a, b):
    K = a.shape[0]
    return np.stack([a.reshape(K, -1, P), b.reshape(K, -1, P)], axis=2).reshape(K, -1)


def _constants():
    c = np.zeros((P, CONST["_"]), np.float32)

    def put(name, a):
        o = CONST[name][0]
        c[0:a.shape[0], o:o + a.shape[1]] = a

    i, j = np.arange(P)[:, None], np.arange(P)[None, :]
    eight = np.arange(NH)
    put("ident", i == j)
    put("ones", np.ones((P, P)))
    put("half", i // HD == j // HD)
    put("cmask", np.where(j <= i, 0.0, NEG))
    put("lmask", np.where(i <= j, 0.0, NEG))
    put("smask", np.where((i <= j) & (i // STEP == j // STEP), 0.0, NEG))
    put("d8", eight[:, None] == eight)
    put("req", i // STEP == np.arange(REQ))
    put("negwin", np.where(np.arange(240) // STEP == REQ - 1, 0.0, NEG)[None, :])
    put("r16", i[:STEP] == j % STEP)
    put("m16", np.where(j[:, :STEP] <= i[:STEP], 0.0, NEG))
    put("sel", eight[:, None] == np.repeat(eight, HD))
    put("nd16", np.where(eight[:, None] == np.repeat(eight, STEP), -1.0, 0.0))
    return c


def kernel(**inputs):
    import concourse.bacc as bacc
    from concourse.bass_utils import run_bass_kernel_spmd

    a = {k: np.asarray(v) for k, v in inputs.items()}
    f32 = np.float32

    par = np.zeros((P, PAR["_"]), f32)

    def put(name, m):
        o = PAR[name][0]
        par[0:m.shape[0], o:o + m.shape[1]] = m

    for l in range(LAYERS):
        put(f"mix{l}", _cols(a["norm_mix_g"][l]))
        put(f"cross{l}", _cols(a["norm_cross_g"][l]))
        put(f"mem{l}", _cols(a["norm_mem_g"][l]))
        put(f"ffn{l}", _cols(a["norm_ffn_g"][l]))
        put(f"xq{l}", a["xa_q_norm_g"][l][:, None])
        put(f"xk{l}", a["xa_k_norm_g"][l][:, None])
    taps = lambda w: w.reshape(w.shape[0], -1, P).transpose(2, 1, 0).reshape(P, -1)
    put("cw", taps(a["conf_dw_w"][0]))
    put("cb", _cols(a["conf_dw_b"][0]))
    put("lng", _cols(a["conf_ln_g"][0]))
    put("lnb", _cols(a["conf_ln_b"][0]))
    put("xw", taps(a["ssd_conv_w"][0]))
    put("xb", _cols(a["ssd_conv_b"][0]))
    put("gn", _cols(a["ssd_norm_g"][0]))
    put("sw", taps(a["sconv_w"][0]))
    put("fq", np.tile(a["fox_q_norm_g"][0], 2)[:, None])
    put("fk", np.tile(a["fox_k_norm_g"][0], 2)[:, None])
    put("dskip", _cols(np.repeat(a["ssd_d"][0], HD)))
    put("dtb", a["ssd_dt_bias"][0][:, None])
    put("alog", a["ssd_a_log"][0][:, None])
    put("fb", a["fox_f_bias"][0][:, None])
    ev, od = a["ev_w_in"][0], a["od_w_in"][0]
    put("wdt", _weights(ev[:, 2560:], NH)[0])
    put("wf", _weights(od[:, 3072:], NH)[0])

    arrays = {
        "par": par,
        "const": _constants(),
        "x": _feature_major(np.concatenate([a["x_prompt"][0], a["x_sample"].reshape(NS, D)])),
        "mem": _feature_major(a["mem_prompt"][0]),
        "conf_state": a["state_conf_conv"][0].reshape(REQ, CW - 1, 4, P).transpose(3, 2, 0, 1),
        "xbc_state": a["state_ssd_conv"][0].reshape(REQ, XW - 1, KD, P).transpose(3, 2, 0, 1),
        "sc_state": a["state_sconv"][0].reshape(REQ, SW - 1, 4, P).transpose(3, 2, 0, 1),
        "ssd_state": a["state_ssd"][0].transpose(3, 0, 1, 2).reshape(P, REQ, 512),
        "fox_k": a["cache_fox_k"][0].reshape(REQ, PAST, 4, P).transpose(0, 3, 2, 1),
        "fox_v": a["cache_fox_v"][0].reshape(REQ, 2, P, 512).transpose(0, 2, 1, 3),
        "fox_logf": a["cache_fox_logf"][0].transpose(2, 0, 1),
        "mem_k": a["cache_mem_k"].reshape(LAYERS, 4, 2, MT, MH, P).transpose(0, 1, 5, 2, 4, 3),
        "mem_v": a["cache_mem_v"].reshape(LAYERS, 4, 2, 2, P, 512).transpose(0, 1, 4, 2, 3, 5),
        "w_glu": _weights(_paired(ev[:, 512:1024], ev[:, 0:512])),
        "w_z": _weights(ev[:, 1024:1536]),
        "w_xbc": _weights(ev[:, 1536:2560]),
        "w_evout": _weights(a["ev_w_out"][0]),
        "w_cgu": _weights(_paired(od[:, 1024:1536], od[:, 0:512])),
        "w_gb": _weights(od[:, 512:1024]),
        "w_fqk": _weights(od[:, 1536:2560]),
        "w_fv": _weights(od[:, 2560:3072]),
        "w_odout": _weights(a["od_w_out"][0]),
    }
    for l in range(LAYERS):
        arrays[f"w_mk{l}"] = _weights(a["xa_wk"][l])
        arrays[f"w_mv{l}"] = _weights(a["xa_wv"][l])
        arrays[f"w_q{l}"] = _weights(a["xa_wq"][l])
        arrays[f"w_wo{l}"] = _weights(a["xa_wo"][l])
        w1 = _weights(_paired(a["ffn_w1"][l], a["ffn_w3"][l]))
        w2 = a["ffn_w2"][l].reshape(2, HALF, P, KD, P).transpose(0, 3, 2, 1, 4).reshape(2, KD, P, HALF * P)
        for i, half in enumerate("ab"):
            arrays[f"w_up{l}{half}"] = w1[i * HALF:(i + 1) * HALF]
            arrays[f"w_down{l}{half}"] = w2[i]
    out_shapes = {
        "o_y": (P, KD, T),
        "o_conf_p": (P, 4, CW - 1), "o_conf_s": (P, 4, REQ, CW - 1),
        "o_xbc_p": (P, KD, XW - 1), "o_xbc_s": (P, KD, REQ, XW - 1),
        "o_ssd_p": (P, 512), "o_ssd_s": (P, REQ, 512),
        "o_sc_p": (P, 4, SW - 1), "o_sc_s": (P, 4, REQ, SW - 1),
        "o_fk": (P, 4, T), "o_fv": (P, NCH, 512), "o_fl": (NH, T),
        "o_mk": (P, LAYERS, MH, MT), "o_mv": (P, LAYERS, 2, 512),
    }
    nc = bacc.Bacc("TRN2", target_bir_lowering=False, num_devices=1)
    arrays = {k: np.ascontiguousarray(v) for k, v in arrays.items()}
    arrays = {f"in_{k}": v for k, v in arrays.items()}
    dram = {k[3:]: nc.dram_tensor(k, v.shape, F32, kind="ExternalInput").ap() for k, v in arrays.items()}
    for k, s in out_shapes.items():
        dram[k] = nc.dram_tensor(k, s, F32, kind="ExternalOutput").ap()
    build(nc, dram)
    r = run_bass_kernel_spmd(nc, [arrays], core_ids=[0]).results[0]
    r = {k: np.asarray(r[k]) for k in out_shapes}

    y = r["o_y"].transpose(2, 1, 0).reshape(T, D)
    prompt_state = lambda s: s.transpose(2, 1, 0).reshape(1, 1, s.shape[2], -1)
    run_state = lambda s: s.transpose(2, 3, 1, 0).reshape(1, REQ, s.shape[3], -1)
    fk = r["o_fk"].transpose(2, 1, 0).reshape(T, NH, HD)
    fv = r["o_fv"].transpose(1, 0, 2).reshape(T, NH, HD)
    fl = r["o_fl"].T
    return tuple(np.ascontiguousarray(v) for v in (
        y[:SEQ].reshape(1, SEQ, D), y[SEQ:].reshape(REQ, STEP, D),
        prompt_state(r["o_conf_p"]), run_state(r["o_conf_s"]),
        prompt_state(r["o_xbc_p"]), run_state(r["o_xbc_s"]),
        r["o_ssd_p"].T.reshape(1, 1, NH, HD, P),
        r["o_ssd_s"].transpose(1, 2, 0).reshape(1, REQ, NH, HD, P),
        prompt_state(r["o_sc_p"]), run_state(r["o_sc_s"]),
        fk[:SEQ].reshape(1, 1, SEQ, NH, HD), fk[SEQ:].reshape(1, REQ, STEP, NH, HD),
        fv[:SEQ].reshape(1, 1, SEQ, NH, HD), fv[SEQ:].reshape(1, REQ, STEP, NH, HD),
        fl[:SEQ].reshape(1, 1, SEQ, NH), fl[SEQ:].reshape(1, REQ, STEP, NH),
        r["o_mk"].transpose(1, 3, 2, 0).reshape(LAYERS, 1, MT, MH, P),
        r["o_mv"].transpose(1, 2, 0, 3).reshape(LAYERS, 1, MT, MH, P),
    ))
```
